# Optimizing a Trainium2 kernel written in Bass

```python
import jax, jax.numpy as jnp
from jax import lax
import numpy as np

D_MODEL = 2048
BATCH = 1
SEQ = 256
DEPTH = 2

CHUNK = 64
EPS = 1e-6
A_BLOCK = 128
A_GROUPS = 4
A_WIDTH = D_MODEL // 2
A_GROUP_DIM = A_WIDTH // A_GROUPS
B_WINDOWS = (2, 4, 8, 16)
B_GROUPS = len(B_WINDOWS)
B_WIDTH = D_MODEL // 2
B_GROUP_DIM = B_WIDTH // B_GROUPS
EVEN_IN = 2 * A_WIDTH + B_WIDTH
EVEN_MIX = A_WIDTH + B_WIDTH
C_HEADS = 16
C_HEAD_DIM = 128
C_WIDTH = C_HEADS * C_HEAD_DIM
Q_BLOCK = 128
ODD_IN = 3 * C_WIDTH + C_HEADS
D_FF = 5632
CONV_WIDTH = 3
N_EVEN = (DEPTH + 1) // 2
N_ODD = DEPTH // 2

kernel_name = 'hybrid_gmlp_pool_fox_encoder'

def rms_norm(x, g):
    x32 = x.astype(jnp.float32)
    y = x32 * lax.rsqrt(jnp.mean(x32 * x32, axis=-1, keepdims=True) + EPS)
    return (y * g.astype(jnp.float32)).astype(x.dtype)

def group_layer_norm(v, g, b):
    v32 = v.astype(jnp.float32)
    mu = jnp.mean(v32, axis=-1, keepdims=True)
    var = jnp.mean(jnp.square(v32 - mu), axis=-1, keepdims=True)
    y = (v32 - mu) * lax.rsqrt(var + EPS) * g.astype(jnp.float32) + b.astype(jnp.float32)
    return y.astype(v.dtype)

def block_causal_mask(n):
    c = jnp.arange(n) // CHUNK
    return c[:, None] >= c[None, :]

def spatial_gating(z, ln_g, ln_b, w_s, b_s):
    bsz, s, _ = z.shape
    u = z[..., :A_WIDTH]
    v = z[..., A_WIDTH:].reshape(bsz, s, A_GROUPS, A_GROUP_DIM)
    v = group_layer_norm(v, ln_g, ln_b)
    v = v.reshape(bsz, s // A_BLOCK, A_BLOCK, A_GROUPS, A_GROUP_DIM)
    w = jnp.where(block_causal_mask(A_BLOCK)[None], w_s, jnp.zeros((), w_s.dtype))
    gate = jnp.einsum('gts,bnsgd->bntgd', w, v) + b_s.T[None, None, :, :, None]
    return u * gate.reshape(bsz, s, A_WIDTH)

def multiscale_pool(p, w_pool, scale):
    bsz, s, _ = p.shape
    p = p.reshape(bsz, s, B_GROUPS, B_GROUP_DIM)
    pos = jnp.arange(s)
    outs = []
    for j, w in enumerate(B_WINDOWS):
        xg = p[:, :, j, :]
        x32 = xg.astype(jnp.float32)
        cs = jnp.cumsum(x32, axis=1)
        lagged = jnp.pad(cs, ((0, 0), (w, 0), (0, 0)))[:, :s]
        count = jnp.minimum(pos + 1, w).astype(jnp.float32)[None, :, None]
        d = ((cs - lagged) / count - x32).astype(p.dtype)
        outs.append(d @ w_pool[j])
    return jnp.concatenate(outs, axis=-1) * scale

def forgetting_attention(q, k, v, log_f):
    bsz, s, h, dh = q.shape
    c = jnp.cumsum(log_f, axis=1).transpose(0, 2, 1)
    scale = dh ** -0.5
    outs = []
    for i in range(s // Q_BLOCK):
        q0 = i * Q_BLOCK
        kl = q0 + Q_BLOCK
        logits = jnp.einsum('bqhd,bkhd->bhqk', q[:, q0:kl], k[:, :kl]).astype(jnp.float32) * scale
        logits = logits + c[:, :, q0:kl, None] - c[:, :, None, :kl]
        causal = (q0 + jnp.arange(Q_BLOCK))[:, None] >= jnp.arange(kl)[None, :]
        logits = jnp.where(causal, logits, -jnp.inf)
        probs = jax.nn.softmax(logits, axis=-1).astype(v.dtype)
        outs.append(jnp.einsum('bhqk,bkhd->bqhd', probs, v[:, :kl]))
    return jnp.concatenate(outs, axis=1)

def conv_ffn(h, w_up, conv_w, conv_b, w_down):
    s = h.shape[1]
    up = h @ w_up
    padded = jnp.pad(up, ((0, 0), (CONV_WIDTH - 1, 0), (0, 0)))
    conv = conv_b
    for j in range(CONV_WIDTH):
        conv = conv + padded[:, j:j + s] * conv_w[j]
    gate, val = conv[..., :D_FF], conv[..., D_FF:]
    return (jax.nn.silu(gate) * val) @ w_down

def setup_inputs(seed: int = 0) -> dict:
    key = jax.random.key(seed)
    ks = jax.random.split(key, 20)
    f32 = jnp.float32

    def nrm(k, shape, scale):
        return jax.random.normal(k, shape, f32) * scale

    return {
        'x': nrm(ks[0], (BATCH, SEQ, D_MODEL), 1.0),
        'norm_mix_g': 1.0 + nrm(ks[1], (DEPTH, D_MODEL), 0.05),
        'norm_ffn_g': 1.0 + nrm(ks[2], (DEPTH, D_MODEL), 0.05),
        'final_norm_g': 1.0 + nrm(ks[3], (D_MODEL,), 0.05),
        'w_in_even': nrm(ks[4], (N_EVEN, D_MODEL, EVEN_IN), D_MODEL ** -0.5),
        'ln_v_g': 1.0 + nrm(ks[5], (N_EVEN, A_GROUPS, A_GROUP_DIM), 0.05),
        'ln_v_b': nrm(ks[6], (N_EVEN, A_GROUPS, A_GROUP_DIM), 0.02),
        'w_spatial': nrm(ks[7], (N_EVEN, A_GROUPS, A_BLOCK, A_BLOCK), A_BLOCK ** -0.5),
        'b_spatial': 1.0 + nrm(ks[8], (N_EVEN, A_GROUPS, A_BLOCK), 0.1),
        'w_pool': nrm(ks[9], (N_EVEN, B_GROUPS, B_GROUP_DIM, B_GROUP_DIM), B_GROUP_DIM ** -0.5),
        'pool_scale': 1.0 + nrm(ks[10], (N_EVEN, B_WIDTH), 0.1),
        'w_out_even': nrm(ks[11], (N_EVEN, EVEN_MIX, D_MODEL), EVEN_MIX ** -0.5),
        'w_in_odd': nrm(ks[12], (N_ODD, D_MODEL, ODD_IN), D_MODEL ** -0.5),
        'b_forget': jax.random.uniform(ks[13], (N_ODD, C_HEADS), f32, 1.0, 5.0),
        'w_out_odd': nrm(ks[14], (N_ODD, C_WIDTH, D_MODEL), C_WIDTH ** -0.5),
        'w_up': nrm(ks[15], (DEPTH, D_MODEL, 2 * D_FF), D_MODEL ** -0.5),
        'conv_w': nrm(ks[16], (DEPTH, CONV_WIDTH, 2 * D_FF), CONV_WIDTH ** -0.5),
        'conv_b': nrm(ks[17], (DEPTH, 2 * D_FF), 0.02),
        'w_down': nrm(ks[18], (DEPTH, D_FF, D_MODEL), D_FF ** -0.5),
    }

def reference(x, norm_mix_g, norm_ffn_g, final_norm_g, w_in_even, ln_v_g, ln_v_b,
              w_spatial, b_spatial, w_pool, pool_scale, w_out_even, w_in_odd,
              b_forget, w_out_odd, w_up, conv_w, conv_b, w_down):
    bsz, s, _ = x.shape
    for i in range(DEPTH):
        h = rms_norm(x, norm_mix_g[i])
        if i % 2 == 0:
            e = i // 2
            p = h @ w_in_even[e]
            z = jax.nn.gelu(p[..., :2 * A_WIDTH], approximate=False)
            y_a = spatial_gating(z, ln_v_g[e], ln_v_b[e], w_spatial[e], b_spatial[e])
            y_b = multiscale_pool(p[..., 2 * A_WIDTH:], w_pool[e], pool_scale[e])
            mix = jnp.concatenate([y_a, y_b], axis=-1) @ w_out_even[e]
        else:
            o = i // 2
            p = h @ w_in_odd[o]
            q = p[..., :C_WIDTH].reshape(bsz, s, C_HEADS, C_HEAD_DIM)
            k = p[..., C_WIDTH:2 * C_WIDTH].reshape(bsz, s, C_HEADS, C_HEAD_DIM)
            v = p[..., 2 * C_WIDTH:3 * C_WIDTH].reshape(bsz, s, C_HEADS, C_HEAD_DIM)
            f_logit = (p[..., 3 * C_WIDTH:] + b_forget[o]).astype(jnp.float32)
            log_f = jax.nn.log_sigmoid(f_logit)
            att = forgetting_attention(q, k, v, log_f).reshape(bsz, s, C_WIDTH)
            mix = att @ w_out_odd[o]
        x = x + mix
        x = x + conv_ffn(rms_norm(x, norm_ffn_g[i]), w_up[i], conv_w[i], conv_b[i], w_down[i])
    return rms_norm(x, final_norm_g)


_drawn_inputs = setup_inputs


def setup_inputs(seed=0):
    import zlib

    import numpy as np

    out = dict(_drawn_inputs(seed))
    spreads = {}
    factors = {'ln_v_g': 3.074, 'ln_v_b': 7.312, 'conv_b': 3.409}
    for name, (base, spread) in spreads.items():
        noise = np.random.default_rng([zlib.crc32(name.encode()), seed]).standard_normal(out[name].shape)
        drawn = base * np.exp(spread * noise) if base else spread * noise
        out[name] = __import__('jax').numpy.asarray(drawn.astype(out[name].dtype))
    for name, factor in factors.items():
        out[name] = (out[name] * factor).astype(out[name].dtype)
    return out
```

```python
from contextlib import ExitStack

import concourse.bass as bass
from concourse import mybir

ALU = mybir.AluOpType
ACT = mybir.ActivationFunctionType
F32 = mybir.dt.float32
F32R = mybir.dt.float32r
AX_X = mybir.AxisListType.X

P = 128
RING = 4
LEAD = 3
PIECE = 2048
KC = 16
TOK = 256
EPS = 1e-6
MASKED = -3.0e38


def at(const, step=0, r=0):
    return const if isinstance(r, int) and r == 0 else r * step + const


def value(eng, expr):
    return expr if isinstance(expr, int) else eng.snap(expr)


def build(nc, x_in, norm_mix_g, norm_ffn_g, final_norm_g, w_in_even, ln_v_g, ln_v_b, w_spatial,
          b_spatial, w_pool, pool_scale, w_out_even, w_in_odd, b_forget, w_out_odd, w_up, conv_w,
          conv_b, w_down, out, c_dram):
    D = x_in.shape[2]
    FF = w_down.shape[1]
    HEADS = b_forget.shape[1]
    FT = FF // P
    GROUP = 4
    NG = FT // GROUP
    AW = D // 2
    AG = ln_v_g.shape[1]
    GD = AW // AG
    assert (D, FF, GD, HEADS) == (2048, 5632, 256, 16) and x_in.shape[1] == TOK

    N_V0 = 0
    N_POOL = 8
    N_U = [16, 19, 21, 23]
    N_WPOOL = 18
    N_OUT0 = 25
    N_FFN = [41, 41 + 132 + 64]
    N_MIX1 = N_FFN[0] + 12 * NG
    N_OUT1 = N_MIX1 + 48
    N_END = N_FFN[1] + 12 * NG
    OUT0_ORDER = [(c, q) for c in range(4) for q in (2, 3, 0, 1)]
    OUT1_ORDER = [(0, 0), (0, 1), (0, 2), (1, 0), (1, 1), (1, 2), (0, 3), (1, 3)] + \
                 [(c, q) for c in (2, 3) for q in range(4)]
    Q_POOL, Q_U, Q_WPOOL = 0, [4, 9, 10, 11], 5
    Q_FFN = [12, 12 + 4 * NG + 16]
    Q_MIX1 = 12 + 4 * NG
    A_OUT0, A_FFN, A_OUT1 = 0, [4, 4 + 4 * NG + 4], 4 + 4 * NG

    def by_rows(w):
        return w.rearrange("(k p) n -> p k n", p=P)

    GAIN = [0, 2 * KC, KC, 3 * KC]
    X_READY = [0, A_OUT0, A_FFN[0] + 4 * (NG - 1), A_OUT1, A_FFN[1] + 4 * (NG - 1)]
    Q_READY = [0, Q_FFN[0], Q_MIX1, Q_FFN[1], Q_FFN[1] + 4 * NG]
    FFN_LINKS, HEAD_LINKS = 4, 8

    W_IN0, W_OUT0, W_IN1, W_OUT1 = (by_rows(w[0]) for w in (w_in_even, w_out_even, w_in_odd, w_out_odd))
    W_UP = [by_rows(w_up[l]) for l in range(2)]
    W_DOWN = [by_rows(w_down[l]) for l in range(2)]
    W_POOL = w_pool[0].rearrange("g (k p) n -> p (g k) n", p=P)
    X_IN = x_in[0].rearrange("(t p) d -> p t d", p=P)
    OUT = out[0].rearrange("(t p) d -> p t d", p=P)

    with ExitStack() as ctx:
        def sb(name, shape, dt=F32):
            return ctx.enter_context(nc.sbuf_tensor(name, shape, dt))

        def sem(name):
            return ctx.enter_context(nc.semaphore(name))

        psT = ctx.enter_context(nc.psum_tensor("ps_turned", [P, 4, 512], F32))
        psA = ctx.enter_context(nc.psum_tensor("ps_straight", [P, 4, 512], F32))

        x = sb("x", [P, 2, D])
        H = sb("h_split", [P, KC, 2 * TOK], F32R)
        Y = sb("y_split", [P, KC, 2 * TOK], F32R)
        raw = sb("w_raw", [P, RING, PIECE])
        wh = sb("w_high", [P, RING, PIECE], F32R)
        wl = sb("w_low", [P, RING, PIECE], F32R)
        wf_split = sb("wf_split", [P, 2, KC * HEADS], F32R)
        cols = sb("feature_columns", [P, 88])
        taps = sb("conv_columns", [P, 2, 4, 2 * FT])
        ident = sb("ident", [P, P])
        ones = sb("ones", [P, P])
        rstdT = sb("rstd_rows", [P, TOK])
        diag = sb("diag", [P, 2, P])
        small = sb("small", [P, 160])
        causal = sb("causal", [P, P])
        work = sb("work", [P, 5760])

        ssq = small[:, 0:8].rearrange("p (t n) -> p t n", t=2)
        ms, sd, rr, nt = (small[:, 8 + 2 * i:10 + 2 * i] for i in range(4))
        rstd = small[:, 16:18]
        vsum, vmu, vsq, vvar, vsd, vrr, vnt = (small[:, 24 + 8 * i:32 + 8 * i] for i in range(7))
        rmax, nmax, rsum, rinv = (small[:, 80 + 2 * i:82 + 2 * i] for i in range(4))
        cq = small[:, 88:120].rearrange("p (t h) -> p t h", t=2)
        inv_count = small[:, 120:136]

        spare = work[:, 3584:4096].rearrange("p (m t) -> p m t", m=2)
        z = work[:, 0:2048].rearrange("p (t d) -> p t d", t=2)
        rows = work[0:88, 0:128]
        conv_rows = work[0:2 * FT, 128:1152].rearrange("p (l j c) -> p l j c", l=2, j=4)
        WT = work[:, 2048:2560].rearrange("p (g t) -> p g t", g=AG)
        WTsum = work[:, 2560:3072].rearrange("p (g t) -> p g t", g=AG)
        bs = work[:, 3072:3584].rearrange("p (g t) -> p g t", g=AG)
        pp, pa, pb = (work[:, 4096 + 544 * i:4640 + 544 * i].rearrange("p (m t) -> p m t", m=2) for i in range(3))
        w_sp = work[:, 4640:5152].rearrange("p (g s) -> p g s", g=AG)
        ub = work[:, 4640:5152].rearrange("p (m t) -> p m t", m=2)
        gt = work[:, 5184:5696].rearrange("p (m t) -> p m t", m=2)
        up = work[:, 0:516].rearrange("p (m t) -> p m t", m=2)
        cc = [work[:, 516 + 512 * i:1028 + 512 * i].rearrange("p (m t) -> p m t", m=2) for i in range(2)]
        act = work[:, 1540:2052].rearrange("p (m t) -> p m t", m=2)
        v = work[:, 0:1024].rearrange("p (t d) -> p t d", t=2)
        qk = [[work[:, 1024 + 1024 * b + 512 * i:1536 + 1024 * b + 512 * i].rearrange("p (m t) -> p m t", m=2)
               for i in range(2)] for b in range(2)]
        probsT = work[:, 3072:3456]
        bf = work[:, 3456:3472]
        bias = work[:, 4096:4864].rearrange("p (h k) -> p h k", h=2)
        cneg = work[0:HEADS, 4096:4352]
        probs = work[:, 4864:5248]
        wf_raw = work[:, 4864:5120]
        q_rstdT = work[:, 5248:5504]
        tri = work[:, 5504:5632]
        fl, fe, lf = (work[:, 5632 + 32 * i:5664 + 32 * i].rearrange("p (t h) -> p t h", t=2) for i in range(3))
        final_g = work[:, 0:2048]

        s_raw = [sem(f"raw_landed{i}") for i in range(RING)]
        s_x = [sem(f"x_landed{i}") for i in range(4)]
        s_rows = sem("rows_landed")
        s_conv = sem("conv_rows_landed")
        s_sp = sem("spatial_landed")
        s_bs = sem("spatial_bias_landed")
        s_wf = sem("forget_weights_landed")
        s_fg = sem("final_gain_landed")
        s_high = sem("high_ready")
        s_low = sem("low_ready")
        s_used = sem("piece_used")
        s_const = sem("constants_ready")
        s_vec = sem("vectors_turned")
        s_cols = sem("columns_ready")
        s_spT = sem("spatial_turned")
        s_WT = sem("spatial_weights_ready")
        s_wsum = sem("spatial_sums_done")
        s_wsr = sem("spatial_sums_read")
        s_wp = sem("pool_product_done")
        s_turn = sem("x_turned")
        s_turn_hi = sem("turned_high")
        s_turned = sem("h_ready")
        s_sq = sem("squares_summed")
        s_ms = sem("mean_square_ready")
        s_sd = sem("root_ready")
        s_diag = sem("diag_ready")
        s_bc = sem("rstd_spread")
        s_rstd = sem("rstd_ready")
        s_spare = sem("low_half_copied")
        s_added = sem("panel_added")
        s_xadd = sem("x_added")
        s_z = sem("z_ready")
        s_mu = sem("z_mean_ready")
        s_zsq = sem("z_squares")
        s_var = sem("z_var_ready")
        s_zsd = sem("z_root_ready")
        s_zn = sem("z_normed")
        s_p = sem("pooled")
        s_phi = sem("pooled_high")
        s_plo = sem("pooled_low")
        s_ybhi = sem("yb_high")
        s_yblo = sem("yb_low")
        s_gate = sem("gates_summed")
        s_u = sem("u_ready")
        s_gelu = sem("u_gelu")
        s_ya = sem("ya_ready")
        s_yahi = sem("ya_high")
        s_yalo = sem("ya_low")
        s_up = sem("up_ready")
        s_tap = sem("last_tap_done")
        s_conved = sem("conv_done")
        s_silu = sem("silu_done")
        s_act = sem("act_ready")
        s_acthi = sem("act_high")
        s_actlo = sem("act_low")
        s_wfs = sem("forget_weights_split")
        s_f = sem("forget_summed")
        s_fl = sem("forget_logits")
        s_fe = sem("forget_exps")
        s_lf = sem("log_forget_ready")
        s_c = sem("c_summed")
        s_cq = sem("c_ready")
        s_cd = sem("c_stored")
        s_bl = sem("bias_landed")
        s_bias = sem("bias_ready")
        s_vr = sem("v_ready")
        s_qk = sem("qk_ready")
        s_sc = sem("scores_done")
        s_scr = sem("scores_read")
        s_mx = sem("row_max_ready")
        s_exp = sem("exp_done")
        s_pr = sem("probs_ready")
        s_pt = sem("probs_turned")
        s_ptc = sem("probs_turned_copied")
        s_att = sem("att_done")
        s_atthi = sem("att_high")
        s_attlo = sem("att_low")
        s_fin = sem("final_ready")
        s_out = sem("out_stored")
        s_vc = sem("vector_chain")
        s_ac = sem("scalar_chain")

        def quad(w, q, c):
            return w[:, 4 * q:4 * q + 4, 512 * c:512 * c + 512]

        def half(w, k, c):
            return w[:, 8 * k:8 * k + 8, c:c + 256]

        block = ctx.enter_context(nc.Block())

        @block.sync
        def _(sp):
            def load(c, src, r=0):
                if not (isinstance(r, int) and c < RING):
                    sp.wait_ge(s_low, at(c - RING + 1, 12, r))
                kk = src.shape[1]
                sp.dma_start(raw[:, c % RING, :].rearrange("p (k n) -> p k n", k=kk), src)\
                    .then_inc(s_raw[c % RING], 16)

            for n in range(4):
                sp.dma_start(x[:, :, 512 * n:512 * n + 512], X_IN[:, :, 512 * n:512 * n + 512]).then_inc(s_x[n], 16)
            for c in range(2):
                for q in range(4):
                    load(N_V0 + 4 * c + q, quad(W_IN0, q, 2 + c))
            for j in range(4):
                for k in range(2):
                    load(N_POOL + 2 * j + k, half(W_IN0, k, 2 * AW + 256 * j))
            for j in range(4):
                for k in range(2):
                    load(N_U[j] + k, half(W_IN0, k, 256 * j))
                if j == 0:
                    load(N_WPOOL, W_POOL)
            for n, (c, q) in enumerate(OUT0_ORDER):
                load(N_OUT0 + n, quad(W_OUT0, q, c))

            def load_ffn(l):
                B = N_FFN[l]

                def panels(c, g, pair, r=0):
                    for j, first in enumerate((0, FF)):
                        for k in range(2):
                            col = value(sp, at(512 * g + 256 * pair + first, 512, r))
                            load(c + 2 * j + k, W_UP[l][:, 8 * k:8 * k + 8, bass.ds(col, 256)], r)

                def down(c, g, r=0):
                    row = value(sp, at(4 * g, 4, r))
                    for n in range(4):
                        load(c + n, W_DOWN[l][:, bass.ds(row, 4), 512 * n:512 * n + 512], r)

                panels(B, 0, 0)
                panels(B + 4, 0, 1)
                with sp.Fori(0, NG - 2) as r:
                    panels(B + 8, 1, 0, r)
                    down(B + 12, 0, r)
                    panels(B + 16, 1, 1, r)
                panels(B + 116, NG - 1, 0)
                panels(B + 120, NG - 1, 1)
                down(B + 124, NG - 2)
                down(B + 128, NG - 1)

            load_ffn(0)

            def load_heads(r):
                first = N_MIX1 - 12
                col = value(sp, at(2 * D - 512, 512, r))
                for q in range(4):
                    load(first + q, W_IN1[:, 4 * q:4 * q + 4, bass.ds(col, 512)], r)
                for pair in range(2):
                    for j in range(2):
                        col = value(sp, at(256 * pair + D * j - 512, 512, r))
                        for k in range(2):
                            load(first + 4 + 4 * pair + 2 * j + k, W_IN1[:, 8 * k:8 * k + 8, bass.ds(col, 256)], r)

            with sp.Fori(1, 5) as r:
                load_heads(r)
            for n, (c, q) in enumerate(OUT1_ORDER):
                load(N_OUT1 + n, quad(W_OUT1, q, c))
            load_ffn(1)
            for n in range(4):
                sp.wait_ge(s_fin, n + 1)
                sp.dma_start(OUT[:, :, 512 * n:512 * n + 512], x[:, :, 512 * n:512 * n + 512]).then_inc(s_out, 16)
            sp.wait_ge(s_out, 64)

        @block.gpsimd
        def _(pool):
            pool.memset(ident[:, :], 0.0).then_inc(s_const, 1)
            pool.wait_ge(s_const, 1)
            pool.affine_select(out=ident[:, :], in_=ident[:, :], compare_op=ALU.not_equal, fill=1.0, base=0,
                               pattern=[[-1, P]], channel_multiplier=1).then_inc(s_const, 1)
            pool.memset(ones[:, :], 1.0).then_inc(s_const, 1)
            for t in range(15):
                last = pool.memset(inv_count[:, t:t + 1], 1.0 / (t + 1))
            last.then_inc(s_const, 1)
            pool.wait_ge(s_xadd, A_FFN[0] + 1)
            pool.wait_ge(s_const, 4)
            pool.memset(tri, 1.0).then_inc(s_const, 1)
            pool.wait_ge(s_const, 5)
            pool.affine_select(out=tri, in_=tri, compare_op=ALU.is_ge, fill=0.0, base=0,
                               pattern=[[1, P]], channel_multiplier=-1).then_inc(s_const, 1)
            pool.memset(causal[:, :], 0.0).then_inc(s_const, 1)
            pool.wait_ge(s_const, 7)
            pool.affine_select(out=causal[:, :], in_=causal[:, :], compare_op=ALU.is_ge, fill=MASKED, base=0,
                               pattern=[[-1, P]], channel_multiplier=1).then_inc(s_const, 1)
            pool.wait_ge(s_const, 8)
            pool.wait_ge(s_cq, 1)
            pool.dma_start(c_dram, cneg).then_inc(s_cd, 16)
            pool.wait_ge(s_cd, 16)
            diagonal = bias.rearrange("p h (b k) -> p h b k", b=3)[:, :, 0:3:2, :]

            def bias_tile(m, r=0):
                heads = c_dram[bass.ds(value(pool, at(2 * m, 2, r)), 2), :]
                if not (isinstance(r, int) and m == 0):
                    pool.wait_ge(s_scr, at(2 * m, 2, r))
                pool.dma_start(bias[:, :, 0:P], heads[:, 0:P].unsqueeze(0).to_broadcast([P, 2, P]))\
                    .then_inc(s_bl, 16)
                pool.dma_start(bias[:, :, P:3 * P], heads.unsqueeze(0).to_broadcast([P, 2, TOK])).then_inc(s_bl, 16)
                pool.wait_ge(s_bl, at(32 * (m + 1), 32, r))
                for h in range(2):
                    ins = pool.tensor_tensor(diagonal[:, h], diagonal[:, h], causal[:, :].unsqueeze(1).to_broadcast([P, 2, P]), ALU.add)
                ins.then_inc(s_bias, 1)

            bias_tile(0)
            with pool.Fori(0, HEADS // 2 - 1) as r:
                bias_tile(1, r)

        @block.scalar
        def _(a):
            def fenced(ins, s, count):
                ins.then_inc(s, 1)
                a.wait_ge(s, count)

            chain = [0]

            def link(ins):
                chain[0] += 1
                fenced(ins, s_ac, chain[0])

            def high(c, r=0):
                s = c % RING
                if isinstance(r, int) and c >= N_END:
                    return
                a.wait_ge(s_raw[s], at(16 * (c // RING + 1), 16 * 12 // RING, r))
                if not (isinstance(r, int) and c < RING):
                    a.wait_ge(s_used, at(c - RING + 1, 12, r))
                a.activation(wh[:, s, :], raw[:, s, :], ACT.Copy).then_inc(s_high, 1)

            def copy_low_half(q, slot, c, r=0, bank=None):
                if c is not None:
                    a.wait_ge(s_used, at(c + 1, 12, r))
                if not (isinstance(r, int) and q == 0):
                    a.wait_ge(s_added, at(q, 4, r))
                src = psT[:, 2 * slot:2 * slot + 2, TOK:] if bank is None else psA[:, bank:bank + 2, TOK:]
                fenced(a.activation(spare, src, ACT.Copy), s_spare, at(q + 1, 4, r))

            def squares(s, n):
                if s == 0:
                    a.wait_ge(s_x[n], 16)
                else:
                    a.wait_ge(s_xadd, X_READY[s] + n + 1)
                    if n == 0:
                        a.wait_ge(s_added, Q_READY[s])
                for t in range(2):
                    ins = a.activation(spare.rearrange("p m t -> p (m t)"), x[:, t, 512 * n:512 * n + 512], ACT.Square,
                                       accum_out=ssq[:, t, n:n + 1])
                    if t == 0:
                        link(ins)
                fenced(ins, s_sq, 4 * s + n + 1)

            def turned_high(s, n):
                a.wait_ge(s_turn, 4 * s + n + 1)
                for kk in range(4):
                    k = 4 * n + kk
                    ins = a.activation(H[:, k, 0:TOK], psT[:, 2 * (n % 2) + kk // 2, TOK * (kk % 2):TOK * (kk % 2) + TOK],
                                       ACT.Copy, scale=cols[:, GAIN[s] + k:GAIN[s] + k + 1])
                    if kk % 2:
                        fenced(ins, s_turn_hi, 8 * s + 2 * n + kk // 2 + 1)

            def root(s):
                a.wait_ge(s_ms, s + 1)
                fenced(a.activation(sd, ms, ACT.Sqrt), s_sd, s + 1)

            a.dma_start(rows[0:32, :], norm_mix_g.rearrange("l (m p) -> (l m) p", p=P)).then_inc(s_rows, 16)
            a.dma_start(rows[32:64, :], norm_ffn_g.rearrange("l (m p) -> (l m) p", p=P)).then_inc(s_rows, 16)
            a.dma_start(rows[64:72, :], pool_scale[0].rearrange("(m p) -> m p", p=P)).then_inc(s_rows, 16)
            a.dma_start(rows[72:80, :], ln_v_g[0].rearrange("g (m p) -> (g m) p", p=P)).then_inc(s_rows, 16)
            a.dma_start(rows[80:88, :], ln_v_b[0].rearrange("g (m p) -> (g m) p", p=P)).then_inc(s_rows, 16)
            for l in range(2):
                a.dma_start(conv_rows[:, l, 0:3, :], conv_w[l].rearrange("j (m p) -> m j p", p=P)).then_inc(s_conv, 16)
                a.dma_start(conv_rows[:, l, 3, :], conv_b[l].rearrange("(m p) -> m p", p=P)).then_inc(s_conv, 16)
            a.dma_start(w_sp, w_spatial[0].rearrange("g t s -> t g s")).then_inc(s_sp, 16)
            a.dma_start(bs, b_spatial[0:1, :, :].to_broadcast([P, AG, P])).then_inc(s_bs, 16)

            for n in range(4):
                squares(0, n)
            a.wait_ge(s_cols, 1)
            for n in range(4):
                turned_high(0, n)
            for n in range(LEAD):
                high(n)
            root(0)

            def gelu_v(c):
                a.wait_ge(s_used, N_V0 + 4 * c + 4)
                if c == 0:
                    a.wait_ge(s_rstd, 1)
                    a.wait_ge(s_cols, 3)
                for t in range(2):
                    for g in range(2):
                        i = 4 * t + 2 * c + g
                        ins = a.activation(z[:, t, 512 * c + GD * g:512 * c + GD * g + GD],
                                           psA[:, 2 * c + t, GD * g:GD * g + GD], ACT.Gelu,
                                           scale=rstd[:, t:t + 1], accum_out=vsum[:, i:i + 1])
                fenced(ins, s_z, c + 1)

            def z_squares(t):
                a.wait_ge(s_mu, 1)
                for g in range(AG):
                    i = 4 * t + g
                    ins = a.activation(pb[:, 0, 0:GD], z[:, t, GD * g:GD * g + GD], ACT.Square,
                                       bias=vmu[:, i:i + 1], accum_out=vsq[:, i:i + 1])
                    if g < AG - 1:
                        link(ins)
                fenced(ins, s_zsq, t + 1)

            def pooled_high(j):
                a.wait_ge(s_p, j + 1)
                fenced(a.activation(Y[:, 2 * j:2 * j + 2, 0:TOK], pa[:, :, 16:], ACT.Copy), s_phi, j + 1)

            def yb_high(j):
                a.wait_ge(s_added, Q_WPOOL + j + 1)
                for m in range(2):
                    i = 2 * j + m
                    ins = a.activation(Y[:, 8 + i, 0:TOK], ub[:, m, :], ACT.Copy, scale=cols[:, 64 + i:65 + i])
                fenced(ins, s_ybhi, j + 1)

            def gelu_u(j):
                a.wait_ge(s_u, j + 1)
                fenced(a.activation(ub, ub, ACT.Gelu), s_gelu, j + 1)

            def ya_high(j):
                a.wait_ge(s_ya, j + 1)
                if j == 0:
                    a.wait_ge(s_used, N_WPOOL + 1)
                fenced(a.activation(Y[:, 2 * j:2 * j + 2, 0:TOK], ub, ACT.Copy), s_yahi, j + 1)

            for n in range(N_OUT0 + 16):
                k = n - N_OUT0
                if k >= 0 and k % 4 == 1 and k > 4:
                    turned_high(1, k // 4 - 1)
                high(n + LEAD)
                if n in (3, 7):
                    gelu_v(n // 4)
                if n in (8, 9):
                    z_squares(n - 8)
                if n == 10:
                    a.wait_ge(s_var, 1)
                    fenced(a.activation(vsd, vvar, ACT.Sqrt), s_zsd, 1)
                if N_POOL <= n < N_U[0] and n % 2:
                    copy_low_half(Q_POOL + n // 2 - 4, (n // 2) % 2, n)
                if N_POOL + 2 <= n <= N_U[0] and n % 2 == 0:
                    pooled_high(n // 2 - 5)
                if n == N_U[0] + 1:
                    copy_low_half(Q_U[0], 0, n)
                if n == N_WPOOL:
                    for j in range(4):
                        if j < 3:
                            a.wait_ge(s_wp, j + 1)
                        copy_low_half(Q_WPOOL + j, 0, n if j == 3 else None, bank=2 * (j % 2))
                        yb_high(j)
                if n == N_U[1] + 1:
                    gelu_u(0)
                    ya_high(0)
                    copy_low_half(Q_U[1], 1, n)
                    gelu_u(1)
                    ya_high(1)
                if n in (N_U[2] + 1, N_U[3] + 1):
                    j = 2 if n == N_U[2] + 1 else 3
                    copy_low_half(Q_U[j], j % 2, n)
                    gelu_u(j)
                    ya_high(j)
                if k >= 4 and k % 4 == 0:
                    squares(1, k // 4 - 1)

            def scale_last_tap(l, j, g, r=0):
                q = 44 * l + 4 * g + j
                a.wait_ge(s_up, at(q + 1, 4, r))
                if j % 2 == 0 and q >= 2:
                    a.wait_ge(s_act, at(q // 2, 2, r))
                for m in range(2):
                    i = at(2 * (j // 2) + m + 4 * g + FT * (j % 2), 4, r)
                    ins = a.activation(cc[j % 2][:, m, :], up[:, m, 2:], ACT.Identity,
                                       scale=taps[:, l, 2, bass.ds(i, 1)], bias=taps[:, l, 3, bass.ds(i, 1)])
                fenced(ins, s_tap, at(q + 1, 4, r))

            def silu(l, pair, g, r=0):
                q = 44 * l + 4 * g + 2 * pair
                a.wait_ge(s_conved, at(q + 1, 4, r))
                fenced(a.activation(cc[0], cc[0], ACT.Silu), s_silu, at(q // 2 + 1, 2, r))

            def act_high(l, pair, g, free, r=0, to=0):
                i = 22 * l + 2 * g + pair
                a.wait_ge(s_act, at(i + 1, 2, r))
                a.wait_ge(s_used, at(free + 1, 12, r))
                y = 4 * to + 2 * pair
                fenced(a.activation(Y[:, y:y + 2, 0:TOK], act, ACT.Copy), s_acthi, at(i + 1, 2, r))

            def ffn(l):
                B, Q, s = N_FFN[l], Q_FFN[l], 1 + 2 * l
                for k in range(8):
                    if k == 0:
                        squares(s, 3)
                        turned_high(s, 3)
                        root(s)
                    if k in (2, 4, 6):
                        scale_last_tap(l, k // 2 - 1, 0)
                    if k in (3, 7):
                        silu(l, k // 4, 0)
                    if k == 5:
                        act_high(l, 0, 0, B - 1)
                    high(B + k + LEAD)
                    if k % 2:
                        copy_low_half(Q + k // 2, (k // 2) % 2, B + k)
                with a.Fori(0, NG - 2) as r:
                    c = B + 8
                    for k in range(12):
                        if k == 0:
                            scale_last_tap(l, 3, 0, r)
                        if k == 1:
                            act_high(l, 1, 0, c - 5, r)
                        if k in (2, 4):
                            scale_last_tap(l, k // 2 - 1, 1, r)
                        if k == 8:
                            act_high(l, 0, 1, c + 7, r)
                        if k == 10:
                            scale_last_tap(l, 2, 1, r)
                        if k in (3, 11):
                            silu(l, k // 8, 1, r)
                        high(c + k + LEAD, r)
                        if k in (1, 3, 9, 11):
                            j = {1: 0, 3: 1, 9: 2, 11: 3}[k]
                            copy_low_half(Q + 4 + j, j % 2, c + k, r)
                c, g = B + 116, NG - 1
                for k in range(16):
                    if k == 0:
                        scale_last_tap(l, 3, g - 1)
                    if k == 1:
                        act_high(l, 1, g - 1, c - 5)
                    if k in (2, 4, 6, 8):
                        scale_last_tap(l, k // 2 - 1, g)
                    if k in (3, 7):
                        silu(l, k // 4, g)
                    if k == 5:
                        act_high(l, 0, g, c - 5, to=1)
                    if k == 9:
                        act_high(l, 1, g, c - 5, to=1)
                    if k >= 14 and l == 0:
                        turned_high(s + 1, k - 14)
                    high(c + k + LEAD)
                    if k < 8 and k % 2:
                        copy_low_half(Q + 4 * g + k // 2, (k // 2) % 2, c + k)
                    if k == 10 and l == 1:
                        a.wait_ge(s_actlo, 4 * NG)
                        a.dma_start(final_g, final_norm_g.unsqueeze(0).to_broadcast([P, D])).then_inc(s_fg, 16)
                    if k >= 13:
                        squares(s + 1, k - 13)

            ffn(0)

            a.wait_ge(s_added, Q_FFN[0] + 4 * NG)
            a.wait_ge(s_actlo, 22)
            a.dma_start(wf_raw.rearrange("p (k h) -> p k h", k=KC), W_IN1[:, :, 3 * D:3 * D + HEADS]).then_inc(s_wf, 16)
            a.dma_start(bf, b_forget.to_broadcast([P, HEADS])).then_inc(s_wf, 16)

            def head_exp(hh, r=0):
                a.wait_ge(s_mx, at(hh + 1, 4, r))
                a.activation(probs[:, 0:P], probs[:, 0:P], ACT.Exp, bias=nmax[:, 0:1], accum_out=rsum[:, 0:1])
                fenced(a.activation(probs[:, P:3 * P], probs[:, P:3 * P], ACT.Exp, bias=nmax[:, 1:2],
                                    accum_out=rsum[:, 1:2]), s_exp, at(hh + 1, 4, r))

            def head_probsT(hh, bank, r=0):
                a.wait_ge(s_pt, at(hh + 1, 4, r))
                if not (isinstance(r, int) and hh == 0):
                    a.wait_ge(s_att, at(hh, 4, r))
                fenced(a.activation(probsT, bank[:, 0:3 * P], ACT.Copy), s_ptc, at(hh + 1, 4, r))

            def head_high(hh, bank, r=0):
                a.wait_ge(s_att, at(hh + 1, 4, r))
                fenced(a.activation(Y[:, bass.ds(at(hh, 4, r), 1), 0:TOK].rearrange("p a t -> p (a t)"), bank[:, 0:TOK],
                                    ACT.Copy), s_atthi, at(hh + 1, 4, r))

            def heads_of_group(first, r=0):
                c = N_MIX1 + 12 * first
                for k in range(12):
                    hh = 4 * first
                    if first == 0 and k == 0:
                        turned_high(2, 2)
                        squares(2, 3)
                        turned_high(2, 3)
                        root(2)
                        a.wait_ge(s_wf, 32)
                        fenced(a.activation(wf_split[:, 0, :], wf_raw, ACT.Copy), s_wfs, 1)
                    if first == 0 and k == 2:
                        a.wait_ge(s_fl, 1)
                        link(a.activation(fe, fe, ACT.Exp))
                        fenced(a.activation(fe, fe, ACT.Ln, bias=1.0), s_fe, 1)
                    if first and k in (0, 2, 4):
                        head_probsT(hh - 3 + k // 2, psA[:, 3, :], r)
                    if first and k in (1, 3, 5):
                        head_high(hh - 3 + k // 2, psA[:, 3, :], r)
                    if k == 10:
                        head_probsT(hh, psA[:, 3, :], r)
                    if k == 11:
                        head_high(hh, psA[:, 3, :], r)
                    high(c + k + LEAD, r)
                    if k == 5:
                        a.wait_ge(s_used, at(c + 4, 12, r))
                        if first == 0:
                            a.wait_ge(s_rstd, 3)
                        if first:
                            a.wait_ge(s_att, at(hh, 4, r))
                        for t in range(2):
                            ins = a.activation(v[:, t, :], psA[:, t, :], ACT.Copy, scale=rstd[:, t:t + 1])
                        fenced(ins, s_vr, at(first + 1, 1, r))
                    if first and k in (1, 3):
                        head_exp(hh - 2 + k // 2, r)
                    if k in (9, 11):
                        head_exp(hh + (k - 9) // 2, r)
                    if k in (5, 7, 9, 11):
                        j = (k - 5) // 2
                        copy_low_half(Q_MIX1 + 4 * first + j, j % 2, c + k, r)

            heads_of_group(0)
            with a.Fori(0, 3) as r:
                heads_of_group(1, r)
            OB, PB, O14 = psT[:, 3, :], psT[:, 3, :], psT[:, 1, :]
            for k in range(16):
                if k == 0:
                    head_probsT(13, psA[:, 3, :])
                if k == 1:
                    head_high(13, O14)
                if k in (2, 4):
                    head_probsT(13 + k // 2, PB)
                if k in (3, 5):
                    head_high(13 + k // 2, OB)
                if k in (8, 9, 13):
                    turned_high(3, {8: 0, 9: 1, 13: 2}[k])
                high(N_OUT1 + k + LEAD)
                if k in (1, 3):
                    head_exp(14 + k // 2)
                if k in (7, 8, 12):
                    squares(3, {7: 0, 8: 1, 12: 2}[k])
            ffn(1)
            squares(4, 3)
            root(4)

        @block.vector
        def _(ve):
            def fenced(ins, s, count):
                ins.then_inc(s, 1)
                ve.wait_ge(s, count)

            chain = {"n": 0, "r": 0, "step": 0}

            def link(ins):
                chain["n"] += 1
                fenced(ins, s_vc, at(chain["n"], chain["step"], chain["r"]))

            def low(c, r=0):
                if isinstance(r, int) and c >= N_END:
                    return
                s = c % RING
                ve.wait_ge(s_high, at(c + 1, 12, r))
                if not (isinstance(r, int) and c < RING):
                    ve.wait_ge(s_used, at(c - RING + 1, 12, r))
                ve.tensor_tensor(wl[:, s, :], raw[:, s, :], wh[:, s, :].bitcast(F32), ALU.subtract).then_inc(s_low, 1)

            def add_halves(to, q, slot, r=0, bank=None):
                ve.wait_ge(s_spare, at(q + 1, 4, r))
                src = psT[:, 2 * slot:2 * slot + 2, 0:TOK] if bank is None else psA[:, bank:bank + 2, 0:TOK]
                fenced(ve.tensor_tensor(to, src, spare, ALU.add), s_added, at(q + 1, 4, r))

            def per_token(ap, factor):
                return ve.tensor_tensor(ap, ap, factor.unsqueeze(1).to_broadcast([P, 2, TOK]), ALU.mult)

            def split_low(y, src, high_done, count, signal):
                ve.wait_ge(high_done, count)
                fenced(ve.tensor_tensor(Y[:, y:y + 2, TOK:], src, Y[:, y:y + 2, 0:TOK].bitcast(F32), ALU.subtract),
                       signal, count)

            def turned_low(s, n):
                for kk in range(4):
                    k = 4 * n + kk
                    if kk % 2 == 0:
                        ve.wait_ge(s_turn_hi, 8 * s + 2 * n + kk // 2 + 1)
                    ins = ve.scalar_tensor_tensor(
                        out=H[:, k, TOK:], in0=psT[:, 2 * (n % 2) + kk // 2, TOK * (kk % 2):TOK * (kk % 2) + TOK],
                        scalar=cols[:, GAIN[s] + k:GAIN[s] + k + 1], in1=H[:, k, 0:TOK].bitcast(F32),
                        op0=ALU.mult, op1=ALU.subtract)
                fenced(ins, s_turned, 4 * s + n + 1)

            def add_to_x(i, n, c, r=0):
                ve.wait_ge(s_used, at(c + 1, 12, r))
                for t in range(2):
                    xc = x[:, t, 512 * n:512 * n + 512]
                    ins = ve.tensor_tensor(xc, xc, psA[:, 2 * (i % 2) + t, :], ALU.add)
                fenced(ins, s_xadd, at(i + 1, 4, r))

            def mean_square(s):
                ve.wait_ge(s_sq, 4 * s + 4)
                link(ve.tensor_reduce(ms, ssq, AX_X, ALU.add))
                fenced(ve.tensor_scalar(ms, ms, 1.0 / D, EPS, ALU.mult, ALU.add), s_ms, s + 1)

            def refined_rsqrt(out_, var, root_, y, t):
                link(ve.reciprocal(y, root_))
                link(ve.tensor_tensor(t, y, y, ALU.mult))
                link(ve.tensor_tensor(t, t, var, ALU.mult))
                link(ve.tensor_scalar(t, t, -0.5, 1.5, ALU.mult, ALU.add))
                link(ve.tensor_tensor(out_, y, t, ALU.mult))

            def spread_rstd(s):
                ve.wait_ge(s_sd, s + 1)
                refined_rsqrt(rstd, ms, sd, rr, nt)
                for t in range(2):
                    ins = ve.tensor_scalar(diag[:, t, :], ident[:, :], rstd[:, t:t + 1], None, ALU.mult)
                fenced(ins, s_diag, s + 1)

            def take_rstd(s):
                ve.wait_ge(s_bc, s + 1)
                fenced(ve.tensor_copy(rstdT[:, :], psA[:, 3, 0:TOK]), s_rstd, s + 1)

            ve.wait_ge(s_vec, 1)
            fenced(ve.tensor_copy(cols[:, :], psA[:, 0, 0:88]), s_cols, 1)
            for l in range(2):
                ve.wait_ge(s_vec, l + 2)
                fenced(ve.tensor_copy(taps[:, l, :, :], psA[:, 1 + l, 0:4 * 2 * FT].rearrange("p (j m) -> p j m", j=4)),
                       s_cols, l + 2)
            for n in range(4):
                turned_low(0, n)
            for n in range(LEAD):
                low(n)
            mean_square(0)
            spread_rstd(0)
            ve.wait_ge(s_spT, 1)
            ve.wait_ge(s_bs, 16)
            link(ve.tensor_copy(WT, psA[:, 3, :].rearrange("p (g t) -> p g t", g=AG)))
            fenced(ve.memset(WT[64:P, :, 0:64], 0.0), s_WT, 1)
            take_rstd(0)
            ve.wait_ge(s_wsum, 1)
            fenced(ve.tensor_copy(WTsum, psA[:, 2, :].rearrange("p (g t) -> p g t", g=AG)), s_wsr, 1)
            link(ve.memset(pp[:, :, 0:16], 0.0))

            ve.wait_ge(s_const, 4)

            def pool_windows(j):
                W = 2 << j
                add_halves(pp[:, :, 16:], Q_POOL + j, j % 2)
                link(per_token(pp[:, :, 16:], rstdT[:, :]))
                src, bufs = pp, [pb, pa] if j % 2 else [pa, pb]
                if j > 0:
                    ve.wait_ge(s_phi, j)
                for i in range(j + 1):
                    sh, dst = 1 << i, bufs[i % 2]
                    lo = 2 * sh if i < j else 16
                    link(ve.tensor_tensor(dst[:, :, lo:], src[:, :, lo:], src[:, :, lo - sh:272 - sh], ALU.add))
                    src = dst
                assert src is pa
                link(ve.tensor_tensor(pb[:, :, 16:15 + W], pa[:, :, 16:15 + W],
                                      inv_count[:, 0:W - 1].unsqueeze(1).to_broadcast([P, 2, W - 1]), ALU.mult))
                link(ve.scalar_tensor_tensor(out=pa[:, :, 16:], in0=pa[:, :, 16:], scalar=1.0 / W, in1=pp[:, :, 16:],
                                             op0=ALU.mult, op1=ALU.subtract))
                fenced(ve.tensor_tensor(pa[:, :, 16:15 + W], pb[:, :, 16:15 + W], pp[:, :, 16:15 + W], ALU.subtract),
                       s_p, j + 1)

            def yb_low(j):
                ve.wait_ge(s_ybhi, j + 1)
                for m in range(2):
                    i = 2 * j + m
                    ins = ve.scalar_tensor_tensor(out=Y[:, 8 + i, TOK:], in0=ub[:, m, :], scalar=cols[:, 64 + i:65 + i],
                                                  in1=Y[:, 8 + i, 0:TOK].bitcast(F32), op0=ALU.mult, op1=ALU.subtract)
                fenced(ins, s_yblo, j + 1)

            def u_ready(j):
                add_halves(ub, Q_U[j], j % 2)
                fenced(per_token(ub, rstdT[:, :]), s_u, j + 1)

            def gate(j):
                ve.wait_ge(s_gate, 1)
                for m in range(2):
                    i = 2 * j + m
                    both = gt[:, m, :].rearrange("p (b t) -> p b t", b=2)
                    ins = ve.scalar_tensor_tensor(
                        out=both, in0=WTsum[:, j:j + 1, :].to_broadcast([P, 2, P]), scalar=cols[:, 80 + i:81 + i],
                        in1=bs[:, j:j + 1, :].to_broadcast([P, 2, P]), op0=ALU.mult, op1=ALU.add)
                    link(ins)
                for m in range(2):
                    i = 2 * j + m
                    link(ve.scalar_tensor_tensor(
                        out=gt[:, m, :], in0=psA[:, j, TOK * m:TOK * m + TOK],
                        scalar=cols[:, 72 + i:73 + i], in1=gt[:, m, :], op0=ALU.mult, op1=ALU.add))
                ve.wait_ge(s_gelu, j + 1)
                fenced(ve.tensor_tensor(ub, ub, gt, ALU.mult), s_ya, j + 1)

            for n in range(N_OUT0 + 16):
                k = n - N_OUT0
                if k >= 0 and k % 4 == 1 and k > 4:
                    turned_low(1, k // 4 - 1)
                low(n + LEAD)
                if n == 8:
                    ve.wait_ge(s_z, 2)
                    fenced(ve.tensor_scalar(vmu, vsum, -1.0 / GD, None, ALU.mult), s_mu, 1)
                if n == 9:
                    ve.wait_ge(s_zsq, 2)
                    fenced(ve.tensor_scalar(vvar, vsq, 1.0 / GD, EPS, ALU.mult, ALU.add), s_var, 1)
                if n == 11:
                    ve.wait_ge(s_zsd, 1)
                    refined_rsqrt(vrr, vvar, vsd, vrr, vnt)
                    for t in range(2):
                        for g in range(AG):
                            i, zg = 4 * t + g, z[:, t, GD * g:GD * g + GD]
                            ins = ve.tensor_scalar(zg, zg, vmu[:, i:i + 1], vrr[:, i:i + 1], ALU.add, ALU.mult)
                    fenced(ins, s_zn, 1)
                if N_POOL <= n < N_U[0] and n % 2:
                    pool_windows(n // 2 - 4)
                if N_POOL + 2 <= n <= N_U[0] and n % 2 == 0:
                    j = n // 2 - 5
                    split_low(2 * j, pa[:, :, 16:], s_phi, j + 1, s_plo)
                if n == N_U[0] + 1:
                    add_halves(gt, Q_U[0], 0)
                if n == N_WPOOL:
                    for j in range(4):
                        add_halves(ub, Q_WPOOL + j, 0, bank=2 * (j % 2))
                        yb_low(j)
                if n == N_U[1] + 1:
                    fenced(ve.tensor_tensor(ub, gt, rstdT[:, :].unsqueeze(1).to_broadcast([P, 2, TOK]), ALU.mult),
                           s_u, 1)
                    gate(0)
                    split_low(0, ub, s_yahi, 1, s_yalo)
                    u_ready(1)
                    gate(1)
                    split_low(2, ub, s_yahi, 2, s_yalo)
                if n in (N_U[2] + 1, N_U[3] + 1):
                    j = 2 if n == N_U[2] + 1 else 3
                    u_ready(j)
                    gate(j)
                    split_low(2 * j, ub, s_yahi, j + 1, s_yalo)
                if k >= 0 and k % 4 == 3:
                    add_to_x(A_OUT0 + k // 4, k // 4, n)

            def take_up(l, j, g, r=0):
                q = Q_FFN[l] + 4 * g + j
                add_halves(up[:, :, 2:], q, j % 2, r)
                fenced(per_token(up[:, :, 2:], rstdT[:, :]), s_up, at(44 * l + 4 * g + j + 1, 4, r))

            def conv(l, j, g, r=0):
                q, c = 44 * l + 4 * g + j, cc[j % 2]
                ve.wait_ge(s_tap, at(q + 1, 4, r))
                for back in (1, 2):
                    for m in range(2):
                        i = at(2 * (j // 2) + m + 4 * g + FT * (j % 2), 4, r)
                        ins = ve.scalar_tensor_tensor(
                            out=c[:, m, :], in0=up[:, m, 2 - back:TOK + 2 - back],
                            scalar=taps[:, l, 2 - back, bass.ds(i, 1)], in1=c[:, m, :], op0=ALU.mult, op1=ALU.add)
                        if back == 1 and m == 1:
                            link(ins)
                fenced(ins, s_conved, at(q + 1, 4, r))

            def product(l, pair, g, r=0):
                i = 22 * l + 2 * g + pair
                ve.wait_ge(s_silu, at(i + 1, 2, r))
                fenced(ve.tensor_tensor(act, cc[0], cc[1], ALU.mult), s_act, at(i + 1, 2, r))

            def act_low(l, pair, g, r=0, to=0):
                i, y = 22 * l + 2 * g + pair, 4 * to + 2 * pair
                ve.wait_ge(s_acthi, at(i + 1, 2, r))
                fenced(ve.tensor_tensor(Y[:, y:y + 2, TOK:], act, Y[:, y:y + 2, 0:TOK].bitcast(F32), ALU.subtract),
                       s_actlo, at(i + 1, 2, r))

            def ffn(l):
                B, s = N_FFN[l], 1 + 2 * l
                for k in range(8):
                    if k == 0:
                        turned_low(s, 3)
                        link(ve.memset(up[:, :, 0:2], 0.0))
                        mean_square(s)
                        spread_rstd(s)
                    if k in (2, 4, 6):
                        conv(l, k // 2 - 1, 0)
                    if k == 4:
                        product(l, 0, 0)
                    if k == 5:
                        act_low(l, 0, 0)
                    low(B + k + LEAD)
                    if k == 1:
                        take_rstd(s)
                    if k % 2:
                        take_up(l, k // 2, 0)
                with ve.Fori(0, NG - 2) as r:
                    c, before = B + 8, chain["n"]
                    chain.update(r=r, step=FFN_LINKS)
                    for k in range(12):
                        if k == 0:
                            conv(l, 3, 0, r)
                            product(l, 1, 0, r)
                        if k == 1:
                            act_low(l, 1, 0, r)
                        if k in (2, 4):
                            conv(l, k // 2 - 1, 1, r)
                        if k == 4:
                            product(l, 0, 1, r)
                        if k == 8:
                            act_low(l, 0, 1, r)
                        if k == 10:
                            conv(l, 2, 1, r)
                        low(c + k + LEAD, r)
                        if k in (1, 3, 9, 11):
                            take_up(l, {1: 0, 3: 1, 9: 2, 11: 3}[k], 1, r)
                        if 4 <= k < 8:
                            add_to_x(A_FFN[l] + k - 4, k - 4, c + k, r)
                    assert chain["n"] == before + FFN_LINKS
                    chain.update(n=before + FFN_LINKS * (NG - 2), r=0, step=0)
                c, g = B + 116, NG - 1
                for k in range(16):
                    if k == 0:
                        conv(l, 3, g - 1)
                        product(l, 1, g - 1)
                    if k == 1:
                        act_low(l, 1, g - 1)
                    if k in (2, 4, 6, 8):
                        conv(l, k // 2 - 1, g)
                    if k in (4, 8):
                        product(l, k // 4 - 1, g)
                    if k == 5:
                        act_low(l, 0, g, to=1)
                    if k == 9:
                        act_low(l, 1, g, to=1)
                    if k >= 14 and l == 0:
                        turned_low(s + 1, k - 14)
                    low(c + k + LEAD)
                    if k < 8 and k % 2:
                        take_up(l, k // 2, g)
                    if k >= 8:
                        add_to_x(A_FFN[l] + 4 * (NG - 2) + k - 8, k % 4, c + k)

            ffn(0)

            def take_qk(j, first, r=0):
                q = Q_MIX1 + 4 * first + j
                buf = qk[j // 2][j % 2]
                add_halves(buf, q, j % 2, r)
                fenced(per_token(buf, rstdT[:, :] if j % 2 else q_rstdT), s_qk, at(4 * first + j + 1, 4, r))

            def head_logits(hh, bank, r=0):
                ve.wait_ge(s_sc, at(hh + 1, 4, r))
                ve.wait_ge(s_bias, at(hh // 2 + 1, 2, r))
                if not (isinstance(r, int) and hh == 0):
                    ve.wait_ge(s_pt, at(hh, 4, r))
                for t in range(2):
                    a0, a1 = (0, P) if t == 0 else (P, 3 * P)
                    ins = ve.scalar_tensor_tensor(out=probs[:, a0:a1], in0=bank[:, a0:a1],
                                                  scalar=cq[:, t, bass.ds(at(hh, 4, r), 1)], in1=bias[:, hh % 2, a0:a1],
                                                  op0=ALU.add, op1=ALU.add)
                fenced(ins, s_scr, at(hh + 1, 4, r))
                ve.tensor_reduce(rmax[:, 0:1], probs[:, 0:P], AX_X, ALU.max)
                link(ve.tensor_reduce(rmax[:, 1:2], probs[:, P:3 * P], AX_X, ALU.max))
                fenced(ve.tensor_scalar(nmax, rmax, -1.0, None, ALU.mult), s_mx, at(hh + 1, 4, r))

            def head_probs(hh, r=0):
                ve.wait_ge(s_exp, at(hh + 1, 4, r))
                link(ve.reciprocal(rinv, rsum))
                ve.tensor_scalar(probs[:, 0:P], probs[:, 0:P], rinv[:, 0:1], None, ALU.mult)
                fenced(ve.tensor_scalar(probs[:, P:3 * P], probs[:, P:3 * P], rinv[:, 1:2], None, ALU.mult),
                       s_pr, at(hh + 1, 4, r))

            def head_low(hh, bank, r=0):
                ve.wait_ge(s_atthi, at(hh + 1, 4, r))
                y = bass.ds(at(hh, 4, r), 1)
                fenced(ve.tensor_tensor(Y[:, y, TOK:].rearrange("p a t -> p (a t)"), bank[:, 0:TOK],
                                        Y[:, y, 0:TOK].rearrange("p a t -> p (a t)").bitcast(F32), ALU.subtract),
                       s_attlo, at(hh + 1, 4, r))

            def heads_of_group(first, r=0):
                c, hh = N_MIX1 + 12 * first, 4 * first
                for k in range(12):
                    if first == 0 and k == 0:
                        turned_low(2, 2)
                        turned_low(2, 3)
                        mean_square(2)
                        ve.wait_ge(s_wfs, 1)
                        fenced(ve.tensor_tensor(wf_split[:, 1, :], wf_raw, wf_split[:, 0, :].bitcast(F32), ALU.subtract),
                               s_wfs, 2)
                        spread_rstd(2)
                    if first and k in (1, 3, 5):
                        head_low(hh - 3 + k // 2, psA[:, 3, :], r)
                    if first and k in (1, 3):
                        head_logits(hh - 2 + k // 2, psA[:, 2, :], r)
                    if k == 11:
                        head_low(hh, psA[:, 3, :], r)
                    if k in (9, 11):
                        head_logits(hh + (k - 9) // 2, psA[:, 2, :], r)
                    low(c + k + LEAD, r)
                    if first == 0 and k == 1:
                        take_rstd(2)
                        link(ve.tensor_scalar(q_rstdT, rstdT[:, :], float(P) ** -0.5, None, ALU.mult))
                        ve.wait_ge(s_f, 1)
                        for t in range(2):
                            link(ve.scalar_tensor_tensor(out=fl[:, t, :], in0=psA[:, 2, 16 * t:16 * t + 16],
                                                         scalar=rstd[:, t:t + 1], in1=bf, op0=ALU.mult, op1=ALU.add))
                        fenced(ve.scalar_tensor_tensor(out=fe, in0=fl, scalar=-1.0, in1=fl, op0=ALU.mult, op1=ALU.min),
                               s_fl, 1)
                    if first == 0 and k == 2:
                        ve.wait_ge(s_fe, 1)
                        fenced(ve.scalar_tensor_tensor(out=lf, in0=fl, scalar=0.0, in1=fe, op0=ALU.min, op1=ALU.subtract),
                               s_lf, 1)
                    if first == 0 and k == 3:
                        ve.wait_ge(s_c, 1)
                        link(ve.tensor_copy(cq, psA[:, 2, 0:32].rearrange("p (t h) -> p t h", t=2)))
                        fenced(ve.tensor_scalar(cneg, psA[0:HEADS, 3, 0:TOK], -1.0, None, ALU.mult), s_cq, 1)
                    if first and k in (1, 3):
                        head_probs(hh - 2 + k // 2, r)
                    if k in (9, 11):
                        head_probs(hh + (k - 9) // 2, r)
                    if k in (5, 7, 9, 11):
                        take_qk((k - 5) // 2, first, r)

            heads_of_group(0)
            with ve.Fori(0, 3) as r:
                before = chain["n"]
                chain.update(r=r, step=HEAD_LINKS)
                heads_of_group(1, r)
                assert chain["n"] == before + HEAD_LINKS, chain["n"] - before
                chain.update(n=before + HEAD_LINKS * 3, r=0, step=0)
            for k in range(16):
                if k == 1:
                    head_low(13, psT[:, 1, :])
                if k in (3, 5):
                    head_low(13 + k // 2, psT[:, 3, :])
                if k in (1, 3):
                    head_logits(14 + k // 2, psT[:, 2, :])
                if k in (8, 9, 13):
                    turned_low(3, {8: 0, 9: 1, 13: 2}[k])
                low(N_OUT1 + k + LEAD)
                if k in (1, 3):
                    head_probs(14 + k // 2)
                if k in (6, 7, 11, 15):
                    c = {6: 0, 7: 1, 11: 2, 15: 3}[k]
                    add_to_x(A_OUT1 + c, c, N_OUT1 + k)
            ffn(1)

            mean_square(4)
            ve.wait_ge(s_sd, 5)
            refined_rsqrt(rstd, ms, sd, rr, nt)
            ve.wait_ge(s_fg, 16)
            for n in range(4):
                for t in range(2):
                    xc = x[:, t, 512 * n:512 * n + 512]
                    ins = ve.scalar_tensor_tensor(out=xc, in0=xc, scalar=rstd[:, t:t + 1],
                                                  in1=final_g[:, 512 * n:512 * n + 512], op0=ALU.mult, op1=ALU.mult)
                ins.then_inc(s_fin, 1)

        @block.tensor
        def _(pe):
            def turned_half(c, k, slot, acts, r=0):
                s = c % RING
                hi = wh[:, s, :].rearrange("p (k n) -> p k n", k=8)
                lo = wl[:, s, :].rearrange("p (k n) -> p k n", k=8)
                pe.wait_ge(s_low, at(c + 1, 12, r))
                for m in range(2):
                    bank = psT[:, 2 * slot + m, :]
                    for kk in range(8):
                        K = 8 * k + kk
                        pe.matmul(bank, hi[:, kk, P * m:P * m + P], acts[:, K, :], start=(K == 0), stop=False,
                                  skip_group_check=True)
                        ins = pe.matmul(bank[:, TOK:], lo[:, kk, P * m:P * m + P], acts[:, K, 0:TOK], start=False,
                                        stop=(K == KC - 1), skip_group_check=True)
                ins.then_inc(s_used, 1)

            def straight_quad(c, slot, acts, k0, first, last, r=0):
                s = c % RING
                hi = wh[:, s, :].rearrange("p (k n) -> p k n", k=4)
                lo = wl[:, s, :].rearrange("p (k n) -> p k n", k=4)
                pe.wait_ge(s_low, at(c + 1, 12, r))
                for t in range(2):
                    bank = psA[:, 2 * slot + t, :]
                    for kk in range(4):
                        ah = acts[:, k0 + kk, P * t:P * t + P]
                        al = acts[:, k0 + kk, TOK + P * t:TOK + P * t + P]
                        pe.matmul(bank, ah, hi[:, kk, :], start=(first and kk == 0), stop=False)
                        pe.matmul(bank, ah, lo[:, kk, :], start=False, stop=False)
                        ins = pe.matmul(bank, al, hi[:, kk, :], start=False, stop=(last and kk == 3))
                ins.then_inc(s_used, 1)

            def transpose_x(s, n):
                if n < 2:
                    if s:
                        pe.wait_ge(s_added, Q_READY[s])
                        if s == 3:
                            pe.wait_ge(s_attlo, HEADS)
                else:
                    pe.wait_ge(s_turned, 4 * s + n - 1)
                if s:
                    pe.wait_ge(s_xadd, X_READY[s] + n + 1)
                else:
                    pe.wait_ge(s_x[n], 16)
                for kk in range(4):
                    for t in range(2):
                        at_col = TOK * (kk % 2) + P * t
                        ins = pe.transpose(psT[:, 2 * (n % 2) + kk // 2, at_col:at_col + P],
                                           x[:, t, 512 * n + P * kk:512 * n + P * kk + P], ident[:, :])
                ins.then_inc(s_turn, 1)

            def spread(s):
                pe.wait_ge(s_diag, s + 1)
                for t in range(2):
                    ins = pe.matmul(psA[:, 3, P * t:P * t + P], ones[:, :], diag[:, t, :], start=(t == 0), stop=True,
                                    skip_group_check=True)
                ins.then_inc(s_bc, 1)

            pe.wait_ge(s_const, 3)
            pe.wait_ge(s_rows, 16 * 5)
            pe.transpose(psA[:, 0, 0:88], rows, ident[0:88, 0:88]).then_inc(s_vec, 1)
            for n in range(2):
                transpose_x(0, n)
            pe.wait_ge(s_conv, 16 * 4)
            for l in range(2):
                for j in range(4):
                    ins = pe.transpose(psA[:, 1 + l, 2 * FT * j:2 * FT * j + 2 * FT], conv_rows[:, l, j, :],
                                       ident[0:2 * FT, 0:2 * FT])
                ins.then_inc(s_vec, 1)
            for n in range(2, 4):
                transpose_x(0, n)
            pe.wait_ge(s_sp, 16)
            for g in range(AG):
                ins = pe.transpose(psA[:, 3, P * g:P * g + P], w_sp[:, g, :], ident[:, :])
            ins.then_inc(s_spT, 1)

            for c in range(2):
                for q in range(4):
                    n = N_V0 + 4 * c + q
                    if c == 0:
                        pe.wait_ge(s_turned, q + 1)
                    if n == N_V0:
                        pe.wait_ge(s_cols, 3)
                    if n == N_V0 + 4:
                        pe.wait_ge(s_wsr, 1)
                    straight_quad(n, c, H, 4 * q, q == 0, q == 3)
                    if n == N_V0:
                        pe.wait_ge(s_WT, 1)
                        spread(0)
                        ins = pe.matmul(psA[:, 2, :], ones[:, :], WT.rearrange("p g t -> p (g t)"), start=True, stop=True)
                        ins.then_inc(s_wsum, 1)
            pe.wait_ge(s_turned, 4)
            for j in range(4):
                for k in range(2):
                    if j >= 2 and k == 0:
                        pe.wait_ge(s_added, Q_POOL + j - 1)
                    turned_half(N_POOL + 2 * j + k, k, j % 2, H)
            for j in range(4):
                for k in range(2):
                    if k == 0:
                        pe.wait_ge(s_added, [Q_POOL + 3, Q_POOL + 4, Q_U[0] + 1, Q_U[1] + 1][j])
                    turned_half(N_U[j] + k, k, j % 2, H)
                if j == 0:
                    s = N_WPOOL % RING
                    hi = wh[:, s, :].rearrange("p (k n) -> p k n", k=8)
                    lo = wl[:, s, :].rearrange("p (k n) -> p k n", k=8)
                    pe.wait_ge(s_low, N_WPOOL + 1)
                    pe.wait_ge(s_z, 2)
                    for g in range(4):
                        pe.wait_ge(s_plo, g + 1)
                        if g >= 2:
                            pe.wait_ge(s_added, Q_WPOOL + g - 1)
                        for m in range(2):
                            bank = psA[:, 2 * (g % 2) + m, :]
                            for kk in range(2):
                                K = 2 * g + kk
                                pe.matmul(bank, hi[:, K, P * m:P * m + P], Y[:, K, :], start=(kk == 0), stop=False,
                                          skip_group_check=True)
                                ins = pe.matmul(bank[:, TOK:], lo[:, K, P * m:P * m + P], Y[:, K, 0:TOK], start=False,
                                                stop=(kk == 1), skip_group_check=True)
                        ins.then_inc(s_wp if g < 3 else s_used, 1)
                if j == 1:
                    pe.wait_ge(s_zn, 1)
                    pe.wait_ge(s_added, Q_WPOOL + 4)
                    for g in range(AG):
                        for m in range(2):
                            for b in range(2):
                                c0 = TOK * m + P * b
                                ins = pe.matmul(psA[:, g, c0:c0 + P], z[:, b, GD * g + P * m:GD * g + P * m + P],
                                                WT[:, g, :], start=(c0 == 0), stop=True, skip_group_check=True)
                    ins.then_inc(s_gate, 1)
            for n, (c, q) in enumerate(OUT0_ORDER):
                if n in (0, 4):
                    pe.wait_ge(s_ya, 2 + n // 2)
                if c >= 2 and n % 4 == 0:
                    pe.wait_ge(s_xadd, A_OUT0 + c - 1)
                if c == 0:
                    pe.wait_ge(s_yblo if q >= 2 else s_yalo, 2 * (q % 2) + 2)
                straight_quad(N_OUT0 + n, c % 2, Y, 4 * q, n % 4 == 0, n % 4 == 3)
                if n in (4, 8, 12):
                    transpose_x(1, n // 4 - 1)

            def panel(l, g, j, c, r=0):
                q = Q_FFN[l] + 4 * g + j
                if g or j >= 2 or not isinstance(r, int):
                    pe.wait_ge(s_added, at(q - 1, 4, r))
                for k in range(2):
                    turned_half(c + k, k, j % 2, H, r)

            def down(l, g, c, r=0, frm=0, transposes=False):
                if frm:
                    pe.wait_ge(s_actlo, 22 * l + 2 * g + 2)
                else:
                    pe.wait_ge(s_actlo, at(22 * l + 2 * g + 2, 2, r))
                for n in range(4):
                    i = A_FFN[l] + 4 * g + n
                    pe.wait_ge(s_xadd, at(i - 1, 4, r))
                    straight_quad(c + n, n % 2, Y, 4 * frm, True, True, r)
                    if transposes and n >= 1:
                        transpose_x(2, n - 1)

            def ffn(l):
                B, s = N_FFN[l], 1 + 2 * l
                pe.wait_ge(s_turned, 4 * s + 3)
                turned_half(B, 0, 0, H)
                transpose_x(s, 3)
                pe.wait_ge(s_turned, 4 * s + 4)
                turned_half(B + 1, 1, 0, H)
                spread(s)
                for j in range(1, 4):
                    panel(l, 0, j, B + 2 * j)
                pe.wait_ge(s_rstd, s + 1)
                with pe.Fori(0, NG - 2) as r:
                    panel(l, 1, 0, B + 8, r)
                    panel(l, 1, 1, B + 10, r)
                    down(l, 0, B + 12, r)
                    panel(l, 1, 2, B + 16, r)
                    panel(l, 1, 3, B + 18, r)
                for j in range(4):
                    panel(l, NG - 1, j, B + 116 + 2 * j)
                down(l, NG - 2, B + 124)
                down(l, NG - 1, B + 128, frm=1, transposes=(l == 0))

            ffn(0)

            def scores(hh, bank, group, r=0):
                if isinstance(r, int) and hh == 0:
                    pe.wait_ge(s_cq, 1)
                else:
                    pe.wait_ge(s_scr, at(hh, 4, r))
                pair = (hh // 2) % 2
                pe.wait_ge(s_qk, at(4 * group + 2 * pair + 2, 4, r))
                qT, kT = qk[pair]
                m = hh % 2
                pe.matmul(bank[:, 0:P], qT[:, m, 0:P], kT[:, m, 0:P], start=True, stop=True, skip_group_check=True)
                pe.matmul(bank[:, P:3 * P], qT[:, m, P:TOK], kT[:, m, :], start=False, stop=True,
                          skip_group_check=True).then_inc(s_sc, 1)

            def turn_probs(hh, bank, r=0):
                pe.wait_ge(s_pr, at(hh + 1, 4, r))
                if not (isinstance(r, int) and hh == 0):
                    pe.wait_ge(s_attlo, at(hh, 4, r))
                for b in range(3):
                    ins = pe.transpose(bank[:, P * b:P * b + P], probs[:, P * b:P * b + P], ident[:, :])
                ins.then_inc(s_pt, 1)

            def attend(hh, bank, group, r=0):
                pe.wait_ge(s_ptc, at(hh + 1, 4, r))
                pe.wait_ge(s_vr, at(group + 1, 1, r))
                f = P * (hh % 4)
                pe.matmul(bank[:, 0:TOK], v[:, 0, f:f + P], probsT[:, 0:TOK], start=True, stop=False,
                          skip_group_check=True)
                pe.matmul(bank[:, P:TOK], v[:, 1, f:f + P], probsT[:, TOK:3 * P], start=False, stop=True,
                          skip_group_check=True).then_inc(s_att, 1)

            def forget_sums():
                pe.wait_ge(s_wfs, 2)
                wfh = wf_split[:, 0, :].rearrange("p (k h) -> p k h", k=KC)
                wfl = wf_split[:, 1, :].rearrange("p (k h) -> p k h", k=KC)
                for t in range(2):
                    o = psA[:, 2, HEADS * t:HEADS * t + HEADS]
                    for k in range(KC):
                        ah, al = H[:, k, P * t:P * t + P], H[:, k, TOK + P * t:TOK + P * t + P]
                        pe.matmul(o, ah, wfh[:, k, :], start=(k == 0), stop=False)
                        pe.matmul(o, ah, wfl[:, k, :], start=False, stop=False)
                        ins = pe.matmul(o, al, wfh[:, k, :], start=False, stop=(k == KC - 1))
                ins.then_inc(s_f, 1)

            def cumulate():
                pe.wait_ge(s_lf, 1)
                pe.wait_ge(s_const, 6)
                c0, c1 = psA[:, 2, 0:HEADS], psA[:, 2, HEADS:2 * HEADS]
                pe.matmul(c0, tri, lf[:, 0, :], start=True, stop=True)
                pe.matmul(c1, ones[:, :], lf[:, 0, :], start=True, stop=False)
                pe.matmul(c1, tri, lf[:, 1, :], start=False, stop=True)
                r0, r1 = psA[0:HEADS, 3, 0:P], psA[0:HEADS, 3, P:TOK]
                pe.matmul(r0, lf[:, 0, :], tri, start=True, stop=True)
                pe.matmul(r1, lf[:, 0, :], ones[:, :], start=True, stop=False)
                pe.matmul(r1, lf[:, 1, :], tri, start=False, stop=True).then_inc(s_c, 1)

            SB, AB = psA[:, 2, :], psA[:, 3, :]

            def heads_of_group(first, r=0):
                c, hh = N_MIX1 + 12 * first, 4 * first
                for k in range(12):
                    if k < 4:
                        if first == 0:
                            pe.wait_ge(s_turned, 8 + k + 1)
                            if k == 0:
                                pe.wait_ge(s_xadd, A_FFN[0] + 4 * NG - 1)
                        elif k == 0:
                            pe.wait_ge(s_vr, at(first, 1, r))
                        straight_quad(c + k, 0, H, 4 * k, k == 0, k == 3, r)
                    else:
                        j = (k - 4) // 2
                        q = Q_MIX1 + 4 * first + j
                        if k % 2 == 0:
                            if first or j >= 2:
                                pe.wait_ge(s_added, at(q - 1, 4, r))
                            else:
                                pe.wait_ge(s_turned, 12)
                        turned_half(c + k, k % 2, j % 2, H, r)
                    if first == 0 and k == 0:
                        transpose_x(2, 3)
                    if first == 0 and k == 1:
                        spread(2)
                        forget_sums()
                    if first == 0 and k == 3:
                        cumulate()
                    if first and k in (0, 2, 4):
                        attend(hh - 3 + k // 2, AB, first - 1, r)
                    if first and k in (0, 2):
                        scores(hh - 2 + k // 2, SB, first - 1, r)
                    if first and k in (1, 3):
                        turn_probs(hh - 2 + k // 2, AB, r)
                    if k == 10:
                        attend(hh, AB, first, r)
                    if k in (8, 10):
                        scores(hh + (k - 8) // 2, SB, first, r)
                    if k in (9, 11):
                        turn_probs(hh + (k - 9) // 2, AB, r)

            heads_of_group(0)
            with pe.Fori(0, 3) as r:
                heads_of_group(1, r)
            for n, (c, q) in enumerate(OUT1_ORDER):
                if n == 0:
                    pe.wait_ge(s_vr, 4)
                if n == 3:
                    pe.wait_ge(s_scr, 14)
                    pe.wait_ge(s_ptc, 14)
                if c >= 2 and q == 0:
                    pe.wait_ge(s_xadd, A_OUT1 + c - 1)
                if c < 2:
                    pe.wait_ge(s_attlo, 4 * q + 4)
                straight_quad(N_OUT1 + n, c % 2, Y, 4 * q, q == 0, q == 3)
                if n == 0:
                    pe.wait_ge(s_qk, 16)
                    attend(13, psT[:, 1, :], 3)
                if n in (0, 2):
                    scores(14 + n // 2, psT[:, 2, :], 3)
                if n in (1, 3):
                    turn_probs(14 + n // 2, psT[:, 3, :])
                if n in (2, 4):
                    attend(13 + n // 2, psT[:, 3, :], 3)
                if n in (7, 8, 12):
                    transpose_x(3, {7: 0, 8: 1, 12: 2}[n])
            ffn(1)


NAMES = ["x", "norm_mix_g", "norm_ffn_g", "final_norm_g", "w_in_even", "ln_v_g", "ln_v_b", "w_spatial", "b_spatial",
         "w_pool", "pool_scale", "w_out_even", "w_in_odd", "b_forget", "w_out_odd", "w_up", "conv_w", "conv_b", "w_down"]


def kernel(**inputs):
    import numpy as np
    import concourse.bacc as bacc
    from concourse.bass_utils import run_bass_kernel_spmd

    nc = bacc.Bacc("TRN2", target_bir_lowering=False, num_devices=1)
    arrays, args = {}, []
    for name in NAMES:
        a = np.ascontiguousarray(inputs[name])
        arrays[f"in_{name}"] = a
        args.append(nc.dram_tensor(f"in_{name}", a.shape, mybir.dt.from_np(a.dtype), kind="ExternalInput").ap())
    result = nc.dram_tensor("result", arrays["in_x"].shape, F32, kind="ExternalOutput").ap()
    c_dram = nc.dram_tensor("c_rows", (arrays["in_b_forget"].shape[1], arrays["in_x"].shape[1]), F32,
                            kind="Internal").ap()
    build(nc, *args, result, c_dram)
    r = run_bass_kernel_spmd(nc, [arrays], core_ids=[0])
    return r.results[0]["result"]
```

```python
from contextlib import ExitStack

import concourse.bass as bass
from concourse import mybir

ALU = mybir.AluOpType
ACT = mybir.ActivationFunctionType
F32 = mybir.dt.float32
F32R = mybir.dt.float32r
AX_X = mybir.AxisListType.X

P = 128
RING = 4
LEAD = 3
PIECE = 2048
KC = 16
TOK = 256
EPS = 1e-6
MASKED = -3.0e38


def at(const, step=0, r=0):
    return const if isinstance(r, int) and r == 0 else r * step + const


def value(eng, expr):
    return expr if isinstance(expr, int) else eng.snap(expr)


def build(nc, x_in, norm_mix_g, norm_ffn_g, final_norm_g, w_in_even, ln_v_g, ln_v_b, w_spatial,
          b_spatial, w_pool, pool_scale, w_out_even, w_in_odd, b_forget, w_out_odd, w_up, conv_w,
          conv_b, w_down, out, c_dram):
    D = x_in.shape[2]
    FF = w_down.shape[1]
    HEADS = b_forget.shape[1]
    FT = FF // P
    GROUP = 4
    NG = FT // GROUP
    AW = D // 2
    AG = ln_v_g.shape[1]
    GD = AW // AG
    assert (D, FF, GD, HEADS) == (2048, 5632, 256, 16) and x_in.shape[1] == TOK

    N_V0 = 0
    N_POOL = 8
    N_U = [(16, 17), (18, 20), (21, 22), (23, 24)]
    N_WPOOL = 19
    N_GATE = [20, 21, 22, 24]
    N_OUT0 = 25
    N_FFN = [41, 41 + 132 + 64]
    N_MIX1 = N_FFN[0] + 12 * NG
    N_OUT1 = N_MIX1 + 48
    N_END = N_FFN[1] + 12 * NG
    OUT0_ORDER = [(c, q) for c in range(4) for q in (2, 3, 0, 1)]
    OUT1_ORDER = [(0, 0), (0, 1), (0, 2), (1, 0), (1, 1), (1, 2), (0, 3), (1, 3)] + \
                 [(c, q) for c in (2, 3) for q in range(4)]
    Q_POOL, Q_U, Q_WPOOL = 0, [4, 9, 10, 11], 5
    Q_FFN = [12, 12 + 4 * NG + 16]
    Q_MIX1 = 12 + 4 * NG
    A_OUT0, A_FFN, A_OUT1 = 0, [4, 4 + 4 * NG + 4], 4 + 4 * NG

    def by_rows(w):
        return w.rearrange("(k p) n -> p k n", p=P)

    GAIN = [0, 2 * KC, KC, 3 * KC]
    X_READY = [0, A_OUT0, A_FFN[0] + 4 * (NG - 1), A_OUT1, A_FFN[1] + 4 * (NG - 1)]
    Q_READY = [0, Q_FFN[0], Q_MIX1, Q_FFN[1], Q_FFN[1] + 4 * NG]
    FFN_LINKS, HEAD_LINKS = 4, 8

    W_IN0, W_OUT0, W_IN1, W_OUT1 = (by_rows(w[0]) for w in (w_in_even, w_out_even, w_in_odd, w_out_odd))
    W_UP = [by_rows(w_up[l]) for l in range(2)]
    W_DOWN = [by_rows(w_down[l]) for l in range(2)]
    W_POOL = w_pool[0].rearrange("g (k p) n -> p (g k) n", p=P)
    X_IN = x_in[0].rearrange("(t p) d -> p t d", p=P)
    OUT = out[0].rearrange("(t p) d -> p t d", p=P)

    with ExitStack() as ctx:
        def sb(name, shape, dt=F32):
            return ctx.enter_context(nc.sbuf_tensor(name, shape, dt))

        def sem(name):
            return ctx.enter_context(nc.semaphore(name))

        psT = ctx.enter_context(nc.psum_tensor("ps_turned", [P, 4, 512], F32))
        psA = ctx.enter_context(nc.psum_tensor("ps_straight", [P, 4, 512], F32))

        x = sb("x", [P, 2, D])
        H = sb("h_split", [P, KC, 2 * TOK], F32R)
        Y = sb("y_split", [P, KC, 2 * TOK], F32R)
        raw = sb("w_raw", [P, RING, PIECE])
        wh = sb("w_high", [P, RING, PIECE], F32R)
        wl = sb("w_low", [P, RING, PIECE], F32R)
        wf_split = sb("wf_split", [P, 2, KC * HEADS], F32R)
        cols = sb("feature_columns", [P, 88])
        taps = sb("conv_columns", [P, 2, 4, 2 * FT])
        ident = sb("ident", [P, P])
        ones = sb("ones", [P, P])
        rstdT = sb("rstd_rows", [P, TOK])
        diag = sb("diag", [P, 2, P])
        small = sb("small", [P, 160])
        causal = sb("causal", [P, P])
        work = sb("work", [P, 5760])

        ssq = small[:, 0:8].rearrange("p (t n) -> p t n", t=2)
        ms, sd, rr, nt = (small[:, 8 + 2 * i:10 + 2 * i] for i in range(4))
        rstd = small[:, 16:18]
        vsum, vmu, vsq, vvar, vsd, vrr, vnt = (small[:, 24 + 8 * i:32 + 8 * i] for i in range(7))
        rmax, nmax, rsum, rinv = (small[:, 80 + 2 * i:82 + 2 * i] for i in range(4))
        cq = small[:, 88:120].rearrange("p (t h) -> p t h", t=2)
        inv_count = small[:, 120:136]

        spare = work[:, 3584:4096].rearrange("p (m t) -> p m t", m=2)
        z = work[:, 0:2048].rearrange("p (t d) -> p t d", t=2)
        rows = work[0:88, 5184:5312]
        conv_rows = work[0:2 * FT, 2048:3072].rearrange("p (l j c) -> p l j c", l=2, j=4)
        WT = work[:, 2048:2560].rearrange("p (g t) -> p g t", g=AG)
        WTsum = work[:, 2560:3072].rearrange("p (g t) -> p g t", g=AG)
        bs = work[:, 3072:3584].rearrange("p (g t) -> p g t", g=AG)
        pp, pa, pb = (work[:, 4096 + 544 * i:4640 + 544 * i].rearrange("p (m t) -> p m t", m=2) for i in range(3))
        w_sp = work[:, 4640:5152].rearrange("p (g s) -> p g s", g=AG)
        ub = work[:, 4640:5152].rearrange("p (m t) -> p m t", m=2)
        wp_sum = [ub, pp[:, :, 16:]]
        gt = work[:, 5184:5696].rearrange("p (m t) -> p m t", m=2)
        up = work[:, 0:516].rearrange("p (m t) -> p m t", m=2)
        cc = [work[:, 516 + 512 * i:1028 + 512 * i].rearrange("p (m t) -> p m t", m=2) for i in range(2)]
        act = work[:, 1540:2052].rearrange("p (m t) -> p m t", m=2)
        v = work[:, 0:1024].rearrange("p (t d) -> p t d", t=2)
        qk = [[work[:, 1024 + 1024 * b + 512 * i:1536 + 1024 * b + 512 * i].rearrange("p (m t) -> p m t", m=2)
               for i in range(2)] for b in range(2)]
        probsT = work[:, 3072:3456]
        bf = work[:, 3456:3472]
        bias = work[:, 4096:4864].rearrange("p (h k) -> p h k", h=2)
        fT = work[0:HEADS, 4096:4608]
        cneg = work[0:HEADS, 4096:4352]
        probs = work[:, 4864:5248]
        wf_raw = work[:, 4864:5120]
        q_rstdT = work[:, 5248:5504]
        tri = work[:, 5504:5632]
        fl, fe, lf = (work[:, 5632 + 32 * i:5664 + 32 * i].rearrange("p (t h) -> p t h", t=2) for i in range(3))
        final_g = work[:, 0:2048]
        last_g = work[:, 2048:3072].rearrange("p (t d) -> p t d", t=2)

        s_raw = [sem(f"raw_landed{i}") for i in range(RING)]
        s_x = [sem(f"x_landed{i}") for i in range(4)]
        s_gains = sem("mixer_gains_landed")
        s_rows = sem("rows_landed")
        s_conv = sem("conv_rows_landed")
        s_sp = sem("spatial_landed")
        s_bs = sem("spatial_bias_landed")
        s_wf = sem("forget_weights_landed")
        s_fg = sem("final_gain_landed")
        s_high = sem("high_ready")
        s_low = sem("low_ready")
        s_used = sem("piece_used")
        s_const = sem("constants_ready")
        s_vec = sem("vectors_turned")
        s_cols = sem("columns_ready")
        s_spT = sem("spatial_turned")
        s_WT = sem("spatial_weights_ready")
        s_wsum = sem("spatial_sums_done")
        s_wsr = sem("spatial_sums_read")
        s_wp = sem("pool_product_done")
        s_turn = sem("x_turned")
        s_turn_hi = sem("turned_high")
        s_turned = sem("h_ready")
        s_sq = sem("squares_summed")
        s_ms = sem("mean_square_ready")
        s_sd = sem("root_ready")
        s_diag = sem("diag_ready")
        s_bc = sem("rstd_spread")
        s_rstd = sem("rstd_ready")
        s_spare = sem("low_half_copied")
        s_added = sem("panel_added")
        s_xadd = sem("x_added")
        s_z = sem("z_ready")
        s_mu = sem("z_mean_ready")
        s_zsq = sem("z_squares")
        s_var = sem("z_var_ready")
        s_zsd = sem("z_root_ready")
        s_zn = sem("z_normed")
        s_p = sem("pooled")
        s_phi = sem("pooled_high")
        s_plo = sem("pooled_low")
        s_ybhi = sem("yb_high")
        s_yblo = sem("yb_low")
        s_gate = sem("gates_summed")
        s_u = sem("u_ready")
        s_gelu = sem("u_gelu")
        s_ya = sem("ya_ready")
        s_yahi = sem("ya_high")
        s_yalo = sem("ya_low")
        s_up = sem("up_ready")
        s_tap = sem("last_tap_done")
        s_conved = sem("conv_done")
        s_silu = sem("silu_done")
        s_act = sem("act_ready")
        s_acthi = sem("act_high")
        s_actlo = sem("act_low")
        s_wfs = sem("forget_weights_split")
        s_f = sem("forget_summed")
        s_fT = sem("forget_sums_copied")
        s_ft = sem("forget_sums_turned")
        s_fl = sem("forget_logits")
        s_fe = sem("forget_exps")
        s_lf = sem("log_forget_ready")
        s_c = sem("c_summed")
        s_cq = sem("c_ready")
        s_cd = sem("c_stored")
        s_bl = sem("bias_landed")
        s_bias = sem("bias_ready")
        s_vr = sem("v_ready")
        s_qk = sem("qk_ready")
        s_sc = sem("scores_done")
        s_scr = sem("scores_read")
        s_mx = sem("row_max_ready")
        s_exp = sem("exp_done")
        s_pr = sem("probs_ready")
        s_pt = sem("probs_turned")
        s_ptc = sem("probs_turned_copied")
        s_att = sem("att_done")
        s_atthi = sem("att_high")
        s_attlo = sem("att_low")
        s_tile0 = sem("last_sum_tile0_done")
        s_xlast = sem("last_chunk_added")
        s_final = sem("final_rstd_ready")
        s_fin0 = sem("final_tile0_ready")
        s_fin1 = sem("final_tile1_ready")
        s_out = sem("out_stored")
        s_vc = sem("vector_chain")
        s_ac = sem("scalar_chain")

        def quad(w, q, c):
            return w[:, 4 * q:4 * q + 4, 512 * c:512 * c + 512]

        def half(w, k, c):
            return w[:, 8 * k:8 * k + 8, c:c + 256]

        def turned_bank(s, n, kk):
            ps, b = (psA, 0) if n == 3 and s in (1, 3) else (psT, 2 * (n % 2))
            return ps[:, b + kk // 2, TOK * (kk % 2):TOK * (kk % 2) + TOK]

        block = ctx.enter_context(nc.Block())

        @block.sync
        def _(sp):
            def load(c, src, r=0):
                if not (isinstance(r, int) and c < RING):
                    sp.wait_ge(s_low, at(c - RING + 1, 12, r))
                kk = src.shape[1]
                sp.dma_start(raw[:, c % RING, :].rearrange("p (k n) -> p k n", k=kk), src)\
                    .then_inc(s_raw[c % RING], 16)

            for c in range(2):
                for q in range(4):
                    if c == 0:
                        sp.dma_start(x[:, :, 512 * q:512 * q + 512], X_IN[:, :, 512 * q:512 * q + 512])\
                            .then_inc(s_x[q], 16)
                    load(N_V0 + 4 * c + q, quad(W_IN0, q, 2 + c))
                if c == 0:
                    sp.dma_start(rows[32:64, :], norm_ffn_g.rearrange("l (m p) -> (l m) p", p=P)).then_inc(s_rows, 16)
                    sp.dma_start(rows[64:72, :], pool_scale[0].rearrange("(m p) -> m p", p=P)).then_inc(s_rows, 16)
                    sp.dma_start(rows[72:80, :], ln_v_g[0].rearrange("g (m p) -> (g m) p", p=P)).then_inc(s_rows, 16)
                    sp.dma_start(rows[80:88, :], ln_v_b[0].rearrange("g (m p) -> (g m) p", p=P)).then_inc(s_rows, 16)
                    for l in range(2):
                        sp.dma_start(conv_rows[:, l, 0:3, :], conv_w[l].rearrange("j (m p) -> m j p", p=P))\
                            .then_inc(s_conv, 16)
                        sp.dma_start(conv_rows[:, l, 3, :], conv_b[l].rearrange("(m p) -> m p", p=P))\
                            .then_inc(s_conv, 16)
                    sp.dma_start(w_sp, w_spatial[0].rearrange("g t s -> t g s")).then_inc(s_sp, 16)
                    sp.dma_start(bs, b_spatial[0:1, :, :].to_broadcast([P, AG, P])).then_inc(s_bs, 16)
            for j in range(4):
                for k in range(2):
                    load(N_POOL + 2 * j + k, half(W_IN0, k, 2 * AW + 256 * j))
            for j in range(4):
                for k in range(2):
                    if N_U[j][k] == N_WPOOL + 1:
                        load(N_WPOOL, W_POOL)
                    load(N_U[j][k], half(W_IN0, k, 256 * j))
            for n, (c, q) in enumerate(OUT0_ORDER):
                load(N_OUT0 + n, quad(W_OUT0, q, c))

            def load_ffn(l):
                B = N_FFN[l]

                def panels(c, g, pair, r=0):
                    for j, first in enumerate((0, FF)):
                        for k in range(2):
                            col = value(sp, at(512 * g + 256 * pair + first, 512, r))
                            load(c + 2 * j + k, W_UP[l][:, 8 * k:8 * k + 8, bass.ds(col, 256)], r)

                def down(c, g, r=0):
                    row = value(sp, at(4 * g, 4, r))
                    for n in range(4):
                        load(c + n, W_DOWN[l][:, bass.ds(row, 4), 512 * n:512 * n + 512], r)

                for k in range(2):
                    for j in range(2):
                        load(B + 2 * k + j, half(W_UP[l], k, FF * j))
                panels(B + 4, 0, 1)
                with sp.Fori(0, NG - 2) as r:
                    panels(B + 8, 1, 0, r)
                    down(B + 12, 0, r)
                    panels(B + 16, 1, 1, r)
                panels(B + 116, NG - 1, 0)
                panels(B + 120, NG - 1, 1)
                down(B + 124, NG - 2)
                down(B + 128, NG - 1)

            load_ffn(0)

            def load_heads(r):
                first = N_MIX1 - 12
                col = value(sp, at(2 * D - 512, 512, r))
                for q in range(4):
                    load(first + q, W_IN1[:, 4 * q:4 * q + 4, bass.ds(col, 512)], r)
                for pair in range(2):
                    for j in range(2):
                        col = value(sp, at(256 * pair + D * j - 512, 512, r))
                        for k in range(2):
                            load(first + 4 + 4 * pair + 2 * j + k, W_IN1[:, 8 * k:8 * k + 8, bass.ds(col, 256)], r)

            with sp.Fori(1, 5) as r:
                load_heads(r)
            for n, (c, q) in enumerate(OUT1_ORDER):
                load(N_OUT1 + n, quad(W_OUT1, q, c))
            load_ffn(1)
            for n in range(4):
                sp.wait_ge(s_fin0, n + 1)
                sp.wait_ge(s_fin1, n + 1)
                sp.dma_start(OUT[:, :, 512 * n:512 * n + 512], x[:, :, 512 * n:512 * n + 512]).then_inc(s_out, 16)
            sp.wait_ge(s_out, 64)

        @block.gpsimd
        def _(pool):
            pool.memset(ident[:, :], 0.0).then_inc(s_const, 1)
            pool.wait_ge(s_const, 1)
            pool.affine_select(out=ident[:, :], in_=ident[:, :], compare_op=ALU.not_equal, fill=1.0, base=0,
                               pattern=[[-1, P]], channel_multiplier=1).then_inc(s_const, 1)
            pool.memset(ones[:, :], 1.0).then_inc(s_const, 1)
            for t in range(15):
                last = pool.memset(inv_count[:, t:t + 1], 1.0 / (t + 1))
            last.then_inc(s_const, 1)
            pool.wait_ge(s_xadd, A_FFN[0] + 1)
            pool.wait_ge(s_const, 4)
            pool.memset(tri, 1.0).then_inc(s_const, 1)
            pool.wait_ge(s_const, 5)
            pool.affine_select(out=tri, in_=tri, compare_op=ALU.is_ge, fill=0.0, base=0,
                               pattern=[[1, P]], channel_multiplier=-1).then_inc(s_const, 1)
            pool.memset(causal[:, :], 0.0).then_inc(s_const, 1)
            pool.wait_ge(s_const, 7)
            pool.affine_select(out=causal[:, :], in_=causal[:, :], compare_op=ALU.is_ge, fill=MASKED, base=0,
                               pattern=[[-1, P]], channel_multiplier=1).then_inc(s_const, 1)
            pool.wait_ge(s_const, 8)
            pool.wait_ge(s_cq, 1)
            pool.dma_start(c_dram, cneg).then_inc(s_cd, 16)
            pool.wait_ge(s_cd, 16)
            diagonal = bias.rearrange("p h (b k) -> p h b k", b=3)[:, :, 0:3:2, :]

            def bias_tile(m, r=0):
                heads = c_dram[bass.ds(value(pool, at(2 * m, 2, r)), 2), :]
                if not (isinstance(r, int) and m == 0):
                    pool.wait_ge(s_scr, at(2 * m, 2, r))
                pool.dma_start(bias[:, :, 0:P], heads[:, 0:P].unsqueeze(0).to_broadcast([P, 2, P]))\
                    .then_inc(s_bl, 16)
                pool.dma_start(bias[:, :, P:3 * P], heads.unsqueeze(0).to_broadcast([P, 2, TOK])).then_inc(s_bl, 16)
                pool.wait_ge(s_bl, at(32 * (m + 1), 32, r))
                for h in range(2):
                    ins = pool.tensor_tensor(diagonal[:, h], diagonal[:, h],
                                             causal[:, :].unsqueeze(1).to_broadcast([P, 2, P]), ALU.add)
                ins.then_inc(s_bias, 1)

            bias_tile(0)
            with pool.Fori(0, HEADS // 2 - 1) as r:
                bias_tile(1, r)

        @block.scalar
        def _(a):
            def fenced(ins, s, count):
                ins.then_inc(s, 1)
                a.wait_ge(s, count)

            chain = [0]

            def link(ins):
                chain[0] += 1
                fenced(ins, s_ac, chain[0])

            def high(c, r=0):
                s = c % RING
                if isinstance(r, int) and c >= N_END:
                    return
                a.wait_ge(s_raw[s], at(16 * (c // RING + 1), 16 * 12 // RING, r))
                if not (isinstance(r, int) and c < RING):
                    a.wait_ge(s_used, at(c - RING + 1, 12, r))
                a.activation(wh[:, s, :], raw[:, s, :], ACT.Copy).then_inc(s_high, 1)

            def copy_low_half(q, slot, c, r=0, bank=None):
                if c is not None:
                    a.wait_ge(s_used, at(c + 1, 12, r))
                if not (isinstance(r, int) and q == 0):
                    a.wait_ge(s_added, at(q, 4, r))
                src = psT[:, 2 * slot:2 * slot + 2, TOK:] if bank is None else psA[:, bank:bank + 2, TOK:]
                fenced(a.activation(spare, src, ACT.Copy), s_spare, at(q + 1, 4, r))

            def squares(s, n):
                if s == 0:
                    a.wait_ge(s_x[n], 16)
                else:
                    a.wait_ge(s_xadd, X_READY[s] + n + 1)
                    if n == 0:
                        a.wait_ge(s_added, Q_READY[s])
                for t in range(2):
                    ins = a.activation(spare.rearrange("p m t -> p (m t)"), x[:, t, 512 * n:512 * n + 512], ACT.Square,
                                       accum_out=ssq[:, t, n:n + 1])
                    if t == 0:
                        link(ins)
                fenced(ins, s_sq, 4 * s + n + 1)

            def turned_high(s, n):
                a.wait_ge(s_turn, 4 * s + n + 1)
                for kk in range(4):
                    k = 4 * n + kk
                    ins = a.activation(H[:, k, 0:TOK], turned_bank(s, n, kk),
                                       ACT.Copy, scale=cols[:, GAIN[s] + k:GAIN[s] + k + 1])
                    if kk % 2:
                        fenced(ins, s_turn_hi, 8 * s + 2 * n + kk // 2 + 1)

            def root(s):
                a.wait_ge(s_ms, s + 1)
                fenced(a.activation(sd, ms, ACT.Sqrt), s_sd, s + 1)

            a.dma_start(rows[0:32, :], norm_mix_g.rearrange("l (m p) -> (l m) p", p=P)).then_inc(s_gains, 16)

            squares(0, 0)
            a.wait_ge(s_cols, 1)
            for n in range(4):
                turned_high(0, n)
                if n < LEAD:
                    high(n)

            def gelu_v(c):
                a.wait_ge(s_used, N_V0 + 4 * c + 4)
                if c == 0:
                    a.wait_ge(s_diag, 1)
                for t in range(2):
                    for g in range(2):
                        i = 4 * t + 2 * c + g
                        ins = a.activation(z[:, t, 512 * c + GD * g:512 * c + GD * g + GD],
                                           psA[:, 2 * c + t, GD * g:GD * g + GD], ACT.Gelu,
                                           scale=rstd[:, t:t + 1], accum_out=vsum[:, i:i + 1])
                fenced(ins, s_z, c + 1)

            def z_squares(t):
                a.wait_ge(s_mu, 1)
                for g in range(AG):
                    i = 4 * t + g
                    ins = a.activation(pb[:, 0, 0:GD], z[:, t, GD * g:GD * g + GD], ACT.Square,
                                       bias=vmu[:, i:i + 1], accum_out=vsq[:, i:i + 1])
                    if g < AG - 1:
                        link(ins)
                fenced(ins, s_zsq, t + 1)

            def pooled_high(j):
                a.wait_ge(s_p, j + 1)
                fenced(a.activation(Y[:, 2 * j:2 * j + 2, 0:TOK], pa[:, :, 16:], ACT.Copy), s_phi, j + 1)

            def yb_high(j):
                a.wait_ge(s_added, Q_WPOOL + j + 1)
                for m in range(2):
                    i = 2 * j + m
                    ins = a.activation(Y[:, 8 + i, 0:TOK], wp_sum[j % 2][:, m, :], ACT.Copy,
                                       scale=cols[:, 64 + i:65 + i])
                fenced(ins, s_ybhi, j + 1)

            def gelu_u(j):
                a.wait_ge(s_u, j + 1)
                fenced(a.activation(ub, ub, ACT.Gelu), s_gelu, j + 1)

            def ya_high(j):
                a.wait_ge(s_ya, j + 1)
                if j == 0:
                    a.wait_ge(s_used, N_WPOOL + 1)
                fenced(a.activation(Y[:, 2 * j:2 * j + 2, 0:TOK], ub, ACT.Copy), s_yahi, j + 1)

            for n in range(N_OUT0 + 16):
                k = n - N_OUT0
                if k >= 0 and k % 4 == 1 and k > 4:
                    turned_high(1, k // 4 - 1)
                high(n + LEAD)
                if n < 2:
                    squares(0, n + 1)
                if n == 1:
                    squares(0, 3)
                if n == 1:
                    root(0)
                if n in (3, 7):
                    gelu_v(n // 4)
                if n in (8, 9):
                    z_squares(n - 8)
                if n == 10:
                    a.wait_ge(s_var, 1)
                    fenced(a.activation(vsd, vvar, ACT.Sqrt), s_zsd, 1)
                if N_POOL <= n < N_POOL + 8 and n % 2:
                    copy_low_half(Q_POOL + n // 2 - 4, (n // 2) % 2, n)
                if N_POOL + 2 <= n <= N_POOL + 8 and n % 2 == 0:
                    pooled_high(n // 2 - 5)
                if n == N_U[0][1]:
                    copy_low_half(Q_U[0], 0, n)
                if n in (N_WPOOL - 1, N_WPOOL):
                    for j in (0, 1) if n < N_WPOOL else (2, 3):
                        if j < 3:
                            a.wait_ge(s_wp, j + 1)
                        copy_low_half(Q_WPOOL + j, 0, n if j == 3 else None, bank=2 * (j % 2))
                    for j in (0, 1) if n < N_WPOOL else (2, 3):
                        yb_high(j)
                if n - 1 in N_GATE:
                    ya_high(N_GATE.index(n - 1))
                if n in N_GATE:
                    j = N_GATE.index(n)
                    if j:
                        copy_low_half(Q_U[j], j % 2, N_U[j][1])
                    gelu_u(j)
                if k >= 4 and k % 4 == 0:
                    squares(1, k // 4 - 1)

            def scale_last_tap(l, j, g, r=0):
                q = 44 * l + 4 * g + j
                a.wait_ge(s_up, at(q + 1, 4, r))
                if j % 2 == 0 and q >= 2:
                    a.wait_ge(s_act, at(q // 2, 2, r))
                for m in range(2):
                    i = at(2 * (j // 2) + m + 4 * g + FT * (j % 2), 4, r)
                    ins = a.activation(cc[j % 2][:, m, :], up[:, m, 2:], ACT.Identity,
                                       scale=taps[:, l, 2, bass.ds(i, 1)], bias=taps[:, l, 3, bass.ds(i, 1)])
                fenced(ins, s_tap, at(q + 1, 4, r))

            def silu(l, pair, g, r=0):
                q = 44 * l + 4 * g + 2 * pair
                a.wait_ge(s_conved, at(q + 1, 4, r))
                fenced(a.activation(cc[0], cc[0], ACT.Silu), s_silu, at(q // 2 + 1, 2, r))

            def act_high(l, pair, g, free, r=0, to=0):
                i = 22 * l + 2 * g + pair
                a.wait_ge(s_act, at(i + 1, 2, r))
                a.wait_ge(s_used, at(free + 1, 12, r))
                y = 4 * to + 2 * pair
                fenced(a.activation(Y[:, y:y + 2, 0:TOK], act, ACT.Copy), s_acthi, at(i + 1, 2, r))

            def ffn(l):
                B, Q, s = N_FFN[l], Q_FFN[l], 1 + 2 * l
                for k in range(8):
                    if k == 0:
                        squares(s, 3)
                        turned_high(s, 3)
                        root(s)
                    high(B + k + LEAD)
                    if k in (3, 4, 6):
                        scale_last_tap(l, {3: 0, 4: 1, 6: 2}[k], 0)
                    if k in (4, 7):
                        silu(l, k // 7, 0)
                    if k == 5:
                        act_high(l, 0, 0, B - 1)
                    if k in (2, 3, 5, 7):
                        j = {2: 0, 3: 1, 5: 2, 7: 3}[k]
                        copy_low_half(Q + j, j % 2, B + k)
                with a.Fori(0, NG - 2) as r:
                    c = B + 8
                    for k in range(12):
                        high(c + k + LEAD, r)
                        if k == 0:
                            scale_last_tap(l, 3, 0, r)
                        if k == 1:
                            act_high(l, 1, 0, c - 5, r)
                        if k in (2, 4):
                            scale_last_tap(l, k // 2 - 1, 1, r)
                        if k == 8:
                            act_high(l, 0, 1, c + 7, r)
                        if k == 10:
                            scale_last_tap(l, 2, 1, r)
                        if k in (3, 11):
                            silu(l, k // 8, 1, r)
                        if k in (1, 3, 9, 11):
                            j = {1: 0, 3: 1, 9: 2, 11: 3}[k]
                            copy_low_half(Q + 4 + j, j % 2, c + k, r)
                c, g = B + 116, NG - 1
                for k in range(16):
                    if k >= 14 and l == 0:
                        turned_high(s + 1, k - 14)
                    high(c + k + LEAD)
                    if k == 0:
                        scale_last_tap(l, 3, g - 1)
                    if k == 1:
                        act_high(l, 1, g - 1, c - 5)
                    if l == 0 and k == 2:
                        a.wait_ge(s_yalo, 4)
                        a.dma_start(wf_raw.rearrange("p (k h) -> p k h", k=KC), W_IN1[:, :, 3 * D:3 * D + HEADS])\
                            .then_inc(s_wf, 16)
                        a.dma_start(bf, b_forget.to_broadcast([P, HEADS])).then_inc(s_wf, 16)
                    if l == 0 and k == 10:
                        a.wait_ge(s_wf, 32)
                        fenced(a.activation(wf_split[:, 0, :], wf_raw, ACT.Copy), s_wfs, 1)
                    if k in (2, 4, 6, 8):
                        scale_last_tap(l, k // 2 - 1, g)
                    if k in (3, 7):
                        silu(l, k // 4, g)
                    if k == 5:
                        act_high(l, 0, g, c - 5, to=1)
                    if k == 9:
                        act_high(l, 1, g, c - 5, to=1)
                    if k < 8 and k % 2:
                        copy_low_half(Q + 4 * g + k // 2, (k // 2) % 2, c + k)
                    if k == 10 and l == 1:
                        a.wait_ge(s_actlo, 4 * NG)
                        a.dma_start(final_g, final_norm_g.unsqueeze(0).to_broadcast([P, D])).then_inc(s_fg, 16)
                    if l == 1 and k == 12:
                        link(a.activation(vsd, vvar, ACT.Sqrt))
                    if k >= 13:
                        squares(s + 1, k - 13)

            ffn(0)

            def head_exp(hh, r=0):
                a.wait_ge(s_mx, at(hh + 1, 4, r))
                a.activation(probs[:, 0:P], probs[:, 0:P], ACT.Exp, bias=nmax[:, 0:1], accum_out=rsum[:, 0:1])
                fenced(a.activation(probs[:, P:3 * P], probs[:, P:3 * P], ACT.Exp, bias=nmax[:, 1:2],
                                    accum_out=rsum[:, 1:2]), s_exp, at(hh + 1, 4, r))

            def head_probsT(hh, bank, r=0):
                a.wait_ge(s_pt, at(hh + 1, 4, r))
                if not (isinstance(r, int) and hh == 0):
                    a.wait_ge(s_att, at(hh, 4, r))
                fenced(a.activation(probsT, bank[:, 0:3 * P], ACT.Copy), s_ptc, at(hh + 1, 4, r))

            def head_high(hh, bank, r=0):
                a.wait_ge(s_att, at(hh + 1, 4, r))
                fenced(a.activation(Y[:, bass.ds(at(hh, 4, r), 1), 0:TOK].rearrange("p a t -> p (a t)"), bank[:, 0:TOK],
                                    ACT.Copy), s_atthi, at(hh + 1, 4, r))

            def heads_of_group(first, r=0):
                c = N_MIX1 + 12 * first
                for k in range(12):
                    hh = 4 * first
                    if first == 0 and k == 0:
                        turned_high(2, 2)
                        squares(2, 3)
                        turned_high(2, 3)
                        root(2)
                    if first == 0 and k == 2:
                        a.wait_ge(s_f, 1)
                        fenced(a.activation(fT, psA[0:HEADS, 2, :], ACT.Copy), s_fT, 1)
                    if first == 0 and k == 3:
                        a.wait_ge(s_fl, 1)
                        link(a.activation(fe, fe, ACT.Exp))
                        fenced(a.activation(fe, fe, ACT.Ln, bias=1.0), s_fe, 1)
                    if first and k in (0, 2, 4):
                        head_probsT(hh - 3 + k // 2, psA[:, 3, :], r)
                    if first and k in (1, 3, 5):
                        head_high(hh - 3 + k // 2, psA[:, 3, :], r)
                    if k == 10:
                        head_probsT(hh, psA[:, 3, :], r)
                    if k == 11:
                        head_high(hh, psA[:, 3, :], r)
                    high(c + k + LEAD, r)
                    if k == 5:
                        a.wait_ge(s_used, at(c + 4, 12, r))
                        if first == 0:
                            a.wait_ge(s_rstd, 3)
                        if first:
                            a.wait_ge(s_att, at(hh, 4, r))
                        for t in range(2):
                            ins = a.activation(v[:, t, :], psA[:, t, :], ACT.Copy, scale=rstd[:, t:t + 1])
                        fenced(ins, s_vr, at(first + 1, 1, r))
                    if first and k in (1, 3):
                        head_exp(hh - 2 + k // 2, r)
                    if k in (9, 11):
                        head_exp(hh + (k - 9) // 2, r)
                    if k in (5, 7, 9, 11):
                        j = (k - 5) // 2
                        copy_low_half(Q_MIX1 + 4 * first + j, j % 2, c + k, r)

            heads_of_group(0)
            with a.Fori(0, 3) as r:
                heads_of_group(1, r)
            OB, PB, O14 = psT[:, 3, :], psT[:, 3, :], psT[:, 1, :]
            for k in range(16):
                if k == 0:
                    head_probsT(13, psA[:, 3, :])
                if k == 1:
                    head_high(13, O14)
                if k in (2, 4):
                    head_probsT(13 + k // 2, PB)
                if k in (3, 5):
                    head_high(13 + k // 2, OB)
                if k in (8, 9, 13):
                    turned_high(3, {8: 0, 9: 1, 13: 2}[k])
                high(N_OUT1 + k + LEAD)
                if k in (1, 3):
                    head_exp(14 + k // 2)
                if k in (7, 8, 12):
                    squares(3, {7: 0, 8: 1, 12: 2}[k])
            ffn(1)
            for t in range(2):
                a.wait_ge(s_xlast, t + 1)
                ins = a.activation(spare.rearrange("p m t -> p (m t)"), x[:, t, D - 512:D], ACT.Square,
                                   accum_out=ssq[:, t, 3:4])
                if t == 0:
                    link(ins)
            fenced(ins, s_sq, 20)
            root(4)
            a.wait_ge(s_final, 1)
            for n in range(4):
                xc = x[:, 1, 512 * n:512 * n + 512]
                a.activation(xc, last_g[:, 1, :] if n == 3 else xc, ACT.Copy, scale=rstd[:, 1:2]).then_inc(s_fin1, 1)

        @block.vector
        def _(ve):
            def fenced(ins, s, count):
                ins.then_inc(s, 1)
                ve.wait_ge(s, count)

            chain = {"n": 0, "r": 0, "step": 0}

            def link(ins):
                chain["n"] += 1
                fenced(ins, s_vc, at(chain["n"], chain["step"], chain["r"]))

            def low(c, r=0):
                if isinstance(r, int) and c >= N_END:
                    return
                s = c % RING
                ve.wait_ge(s_high, at(c + 1, 12, r))
                if not (isinstance(r, int) and c < RING):
                    ve.wait_ge(s_used, at(c - RING + 1, 12, r))
                ve.tensor_tensor(wl[:, s, :], raw[:, s, :], wh[:, s, :].bitcast(F32), ALU.subtract).then_inc(s_low, 1)

            def add_halves(to, q, slot, r=0, bank=None):
                ve.wait_ge(s_spare, at(q + 1, 4, r))
                src = psT[:, 2 * slot:2 * slot + 2, 0:TOK] if bank is None else psA[:, bank:bank + 2, 0:TOK]
                fenced(ve.tensor_tensor(to, src, spare, ALU.add), s_added, at(q + 1, 4, r))

            def per_token(ap, factor):
                return ve.tensor_tensor(ap, ap, factor.unsqueeze(1).to_broadcast([P, 2, TOK]), ALU.mult)

            def split_low(y, src, high_done, count, signal):
                ve.wait_ge(high_done, count)
                fenced(ve.tensor_tensor(Y[:, y:y + 2, TOK:], src, Y[:, y:y + 2, 0:TOK].bitcast(F32), ALU.subtract),
                       signal, count)

            def turned_low(s, n):
                for kk in range(4):
                    k = 4 * n + kk
                    if kk % 2 == 0:
                        ve.wait_ge(s_turn_hi, 8 * s + 2 * n + kk // 2 + 1)
                    ins = ve.scalar_tensor_tensor(
                        out=H[:, k, TOK:], in0=turned_bank(s, n, kk),
                        scalar=cols[:, GAIN[s] + k:GAIN[s] + k + 1], in1=H[:, k, 0:TOK].bitcast(F32),
                        op0=ALU.mult, op1=ALU.subtract)
                fenced(ins, s_turned, 4 * s + n + 1)

            def add_to_x(i, n, c, r=0):
                ve.wait_ge(s_used, at(c + 1, 12, r))
                for t in range(2):
                    xc = x[:, t, 512 * n:512 * n + 512]
                    ins = ve.tensor_tensor(xc, xc, psA[:, 2 * (i % 2) + t, :], ALU.add)
                fenced(ins, s_xadd, at(i + 1, 4, r))

            def mean_square(s):
                ve.wait_ge(s_sq, 4 * s + 4)
                link(ve.tensor_reduce(ms, ssq, AX_X, ALU.add))
                fenced(ve.tensor_scalar(ms, ms, 1.0 / D, EPS, ALU.mult, ALU.add), s_ms, s + 1)

            def refined_rsqrt(out_, var, root_, y, t, last=None):
                link(ve.reciprocal(y, root_))
                link(ve.tensor_tensor(t, y, y, ALU.mult))
                link(ve.tensor_tensor(t, t, var, ALU.mult))
                link(ve.tensor_scalar(t, t, -0.5, 1.5, ALU.mult, ALU.add))
                ins = ve.tensor_tensor(out_, y, t, ALU.mult)
                if last is None:
                    link(ins)
                else:
                    fenced(ins, last, 1)

            def spread_rstd(s):
                ve.wait_ge(s_sd, s + 1)
                refined_rsqrt(rstd, ms, sd, rr, nt)
                for t in range(2):
                    ins = ve.tensor_scalar(diag[:, t, :], ident[:, :], rstd[:, t:t + 1], None, ALU.mult)
                fenced(ins, s_diag, s + 1)

            def take_rstd(s):
                ve.wait_ge(s_bc, s + 1)
                bank = psA[:, 3, :] if s else psT[:, 1, :]
                fenced(ve.tensor_copy(rstdT[:, :], bank[:, 0:TOK]), s_rstd, s + 1)

            ve.wait_ge(s_vec, 1)
            fenced(ve.tensor_copy(cols[:, 0:32], psA[:, 2, 0:32]), s_cols, 1)
            for n in range(4):
                turned_low(0, n)
                if n < LEAD:
                    low(n)

            def spatial_weights():
                for l in range(2):
                    ve.wait_ge(s_vec, l + 2)
                    if l == 0:
                        link(ve.tensor_copy(cols[:, 32:88], psT[:, 2, 8 * FT + 32:8 * FT + 88]))
                    link(ve.tensor_copy(taps[:, l, :, :],
                                        psT[:, 2 + l, 0:4 * 2 * FT].rearrange("p (j m) -> p j m", j=4)))
                ve.wait_ge(s_spT, 1)
                link(ve.tensor_copy(WT, psT[:, 0, :].rearrange("p (g t) -> p g t", g=AG)))
                fenced(ve.memset(WT[64:P, :, 0:64], 0.0), s_WT, 1)

            ve.wait_ge(s_const, 4)

            def pool_windows(j):
                W = 2 << j
                add_halves(pp[:, :, 16:], Q_POOL + j, j % 2)
                link(per_token(pp[:, :, 16:], rstdT[:, :]))
                src, bufs = pp, [pb, pa] if j % 2 else [pa, pb]
                if j > 0:
                    ve.wait_ge(s_phi, j)
                for i in range(j + 1):
                    sh, dst = 1 << i, bufs[i % 2]
                    lo = 2 * sh if i < j else 16
                    link(ve.tensor_tensor(dst[:, :, lo:], src[:, :, lo:], src[:, :, lo - sh:272 - sh], ALU.add))
                    src = dst
                assert src is pa
                link(ve.tensor_tensor(pb[:, :, 16:15 + W], pa[:, :, 16:15 + W],
                                      inv_count[:, 0:W - 1].unsqueeze(1).to_broadcast([P, 2, W - 1]), ALU.mult))
                link(ve.scalar_tensor_tensor(out=pa[:, :, 16:], in0=pa[:, :, 16:], scalar=1.0 / W, in1=pp[:, :, 16:],
                                             op0=ALU.mult, op1=ALU.subtract))
                fenced(ve.tensor_tensor(pa[:, :, 16:15 + W], pb[:, :, 16:15 + W], pp[:, :, 16:15 + W], ALU.subtract),
                       s_p, j + 1)

            def yb_low(j):
                ve.wait_ge(s_ybhi, j + 1)
                for m in range(2):
                    i = 2 * j + m
                    ins = ve.scalar_tensor_tensor(out=Y[:, 8 + i, TOK:], in0=wp_sum[j % 2][:, m, :],
                                                  scalar=cols[:, 64 + i:65 + i],
                                                  in1=Y[:, 8 + i, 0:TOK].bitcast(F32), op0=ALU.mult, op1=ALU.subtract)
                fenced(ins, s_yblo, j + 1)

            def u_ready(j):
                add_halves(ub, Q_U[j], j % 2)
                fenced(per_token(ub, rstdT[:, :]), s_u, j + 1)

            def gate(j):
                ve.wait_ge(s_gate, 1)
                for m in range(2):
                    i = 2 * j + m
                    both = gt[:, m, :].rearrange("p (b t) -> p b t", b=2)
                    ins = ve.scalar_tensor_tensor(
                        out=both, in0=WTsum[:, j:j + 1, :].to_broadcast([P, 2, P]), scalar=cols[:, 80 + i:81 + i],
                        in1=bs[:, j:j + 1, :].to_broadcast([P, 2, P]), op0=ALU.mult, op1=ALU.add)
                    link(ins)
                for m in range(2):
                    i = 2 * j + m
                    link(ve.scalar_tensor_tensor(
                        out=gt[:, m, :], in0=psA[:, j, TOK * m:TOK * m + TOK],
                        scalar=cols[:, 72 + i:73 + i], in1=gt[:, m, :], op0=ALU.mult, op1=ALU.add))
                ve.wait_ge(s_gelu, j + 1)
                fenced(ve.tensor_tensor(ub, ub, gt, ALU.mult), s_ya, j + 1)

            for n in range(N_OUT0 + 16):
                k = n - N_OUT0
                if k >= 0 and k % 4 == 1 and k > 4:
                    turned_low(1, k // 4 - 1)
                low(n + LEAD)
                if n == 1:
                    mean_square(0)
                    spread_rstd(0)
                if n == 4:
                    spatial_weights()
                if n == 5:
                    take_rstd(0)
                if n == 6:
                    ve.wait_ge(s_wsum, 1)
                    fenced(ve.tensor_copy(WTsum, psT[:, 0, :].rearrange("p (g t) -> p g t", g=AG)), s_wsr, 1)
                    link(ve.memset(pp[:, :, 0:16], 0.0))
                    ve.wait_ge(s_bs, 16)
                if n == 8:
                    ve.wait_ge(s_z, 2)
                    fenced(ve.tensor_scalar(vmu, vsum, -1.0 / GD, None, ALU.mult), s_mu, 1)
                if n == 9:
                    ve.wait_ge(s_zsq, 2)
                    fenced(ve.tensor_scalar(vvar, vsq, 1.0 / GD, EPS, ALU.mult, ALU.add), s_var, 1)
                if n == 11:
                    ve.wait_ge(s_zsd, 1)
                    refined_rsqrt(vrr, vvar, vsd, vrr, vnt)
                    for t in range(2):
                        for g in range(AG):
                            i, zg = 4 * t + g, z[:, t, GD * g:GD * g + GD]
                            ins = ve.tensor_scalar(zg, zg, vmu[:, i:i + 1], vrr[:, i:i + 1], ALU.add, ALU.mult)
                    fenced(ins, s_zn, 1)
                if N_POOL <= n < N_POOL + 8 and n % 2:
                    pool_windows(n // 2 - 4)
                if N_POOL + 2 <= n <= N_POOL + 8 and n % 2 == 0:
                    j = n // 2 - 5
                    split_low(2 * j, pa[:, :, 16:], s_phi, j + 1, s_plo)
                if n == N_U[0][1]:
                    add_halves(gt, Q_U[0], 0)
                if n in (N_WPOOL - 1, N_WPOOL):
                    for j in (0, 1) if n < N_WPOOL else (2, 3):
                        add_halves(wp_sum[j % 2], Q_WPOOL + j, 0, bank=2 * (j % 2))
                    for j in (0, 1) if n < N_WPOOL else (2, 3):
                        yb_low(j)
                if n - 1 in N_GATE:
                    j = N_GATE.index(n - 1)
                    split_low(2 * j, ub, s_yahi, j + 1, s_yalo)
                if n in N_GATE:
                    j = N_GATE.index(n)
                    if j == 0:
                        fenced(ve.tensor_tensor(ub, gt, rstdT[:, :].unsqueeze(1).to_broadcast([P, 2, TOK]), ALU.mult),
                               s_u, 1)
                    else:
                        u_ready(j)
                    gate(j)
                if k >= 0 and k % 4 == 3:
                    add_to_x(A_OUT0 + k // 4, k // 4, n)

            def take_up(l, j, g, r=0):
                q = Q_FFN[l] + 4 * g + j
                add_halves(up[:, :, 2:], q, j % 2, r)
                fenced(per_token(up[:, :, 2:], rstdT[:, :]), s_up, at(44 * l + 4 * g + j + 1, 4, r))

            def conv(l, j, g, r=0):
                q, c = 44 * l + 4 * g + j, cc[j % 2]
                ve.wait_ge(s_tap, at(q + 1, 4, r))
                for back in (1, 2):
                    for m in range(2):
                        i = at(2 * (j // 2) + m + 4 * g + FT * (j % 2), 4, r)
                        ins = ve.scalar_tensor_tensor(
                            out=c[:, m, :], in0=up[:, m, 2 - back:TOK + 2 - back],
                            scalar=taps[:, l, 2 - back, bass.ds(i, 1)], in1=c[:, m, :], op0=ALU.mult, op1=ALU.add)
                        if back == 1 and m == 1:
                            link(ins)
                fenced(ins, s_conved, at(q + 1, 4, r))

            def product(l, pair, g, r=0):
                i = 22 * l + 2 * g + pair
                ve.wait_ge(s_silu, at(i + 1, 2, r))
                fenced(ve.tensor_tensor(act, cc[0], cc[1], ALU.mult), s_act, at(i + 1, 2, r))

            def act_low(l, pair, g, r=0, to=0):
                i, y = 22 * l + 2 * g + pair, 4 * to + 2 * pair
                ve.wait_ge(s_acthi, at(i + 1, 2, r))
                fenced(ve.tensor_tensor(Y[:, y:y + 2, TOK:], act, Y[:, y:y + 2, 0:TOK].bitcast(F32), ALU.subtract),
                       s_actlo, at(i + 1, 2, r))

            def ffn(l):
                B, s = N_FFN[l], 1 + 2 * l
                for k in range(8):
                    if k == 0:
                        turned_low(s, 3)
                        link(ve.memset(up[:, :, 0:2], 0.0))
                        mean_square(s)
                        spread_rstd(s)
                    low(B + k + LEAD)
                    if k in (3, 4, 6):
                        conv(l, {3: 0, 4: 1, 6: 2}[k], 0)
                    if k == 4:
                        product(l, 0, 0)
                    if k == 5:
                        act_low(l, 0, 0)
                    if k == 1:
                        take_rstd(s)
                    if k in (2, 3, 5, 7):
                        take_up(l, {2: 0, 3: 1, 5: 2, 7: 3}[k], 0)
                with ve.Fori(0, NG - 2) as r:
                    c, before = B + 8, chain["n"]
                    chain.update(r=r, step=FFN_LINKS)
                    for k in range(12):
                        low(c + k + LEAD, r)
                        if k == 0:
                            conv(l, 3, 0, r)
                            product(l, 1, 0, r)
                        if k == 1:
                            act_low(l, 1, 0, r)
                        if k in (2, 4):
                            conv(l, k // 2 - 1, 1, r)
                        if k == 4:
                            product(l, 0, 1, r)
                        if k == 8:
                            act_low(l, 0, 1, r)
                        if k == 10:
                            conv(l, 2, 1, r)
                        if k in (1, 3, 9, 11):
                            take_up(l, {1: 0, 3: 1, 9: 2, 11: 3}[k], 1, r)
                        if 4 <= k < 8:
                            add_to_x(A_FFN[l] + k - 4, k - 4, c + k, r)
                    assert chain["n"] == before + FFN_LINKS
                    chain.update(n=before + FFN_LINKS * (NG - 2), r=0, step=0)
                c, g = B + 116, NG - 1
                for k in range(16):
                    if k >= 14 and l == 0:
                        turned_low(s + 1, k - 14)
                    low(c + k + LEAD)
                    if k == 0:
                        conv(l, 3, g - 1)
                        product(l, 1, g - 1)
                    if k == 1:
                        act_low(l, 1, g - 1)
                    if k in (2, 4, 6, 8):
                        conv(l, k // 2 - 1, g)
                    if k in (4, 8):
                        product(l, k // 4 - 1, g)
                    if l == 0 and k == 10:
                        ve.wait_ge(s_wfs, 1)
                        fenced(ve.tensor_tensor(wf_split[:, 1, :], wf_raw, wf_split[:, 0, :].bitcast(F32), ALU.subtract),
                               s_wfs, 2)
                    if k == 5:
                        act_low(l, 0, g, to=1)
                    if k == 9:
                        act_low(l, 1, g, to=1)
                    if k < 8 and k % 2:
                        take_up(l, k // 2, g)
                    if l == 1 and k >= 14:
                        times_gain(k - 14)
                    if k >= 8 and not (l == 1 and k == 15):
                        add_to_x(A_FFN[l] + 4 * (NG - 2) + k - 8, k % 4, c + k)

            def times_gain(n):
                if n == 0:
                    ve.wait_ge(s_fg, 16)
                ve.wait_ge(s_sq, 16 + n + 1)
                for t in range(2):
                    xc = x[:, t, 512 * n:512 * n + 512]
                    ins = ve.tensor_tensor(xc, xc, final_g[:, 512 * n:512 * n + 512], ALU.mult)
                link(ins)

            ffn(0)

            def take_qk(j, first, r=0):
                q = Q_MIX1 + 4 * first + j
                buf = qk[j // 2][j % 2]
                add_halves(buf, q, j % 2, r)
                fenced(per_token(buf, rstdT[:, :] if j % 2 else q_rstdT), s_qk, at(4 * first + j + 1, 4, r))

            def head_logits(hh, bank, r=0):
                ve.wait_ge(s_sc, at(hh + 1, 4, r))
                ve.wait_ge(s_bias, at(hh // 2 + 1, 2, r))
                if not (isinstance(r, int) and hh == 0):
                    ve.wait_ge(s_pt, at(hh, 4, r))
                for t in range(2):
                    a0, a1 = (0, P) if t == 0 else (P, 3 * P)
                    ins = ve.scalar_tensor_tensor(out=probs[:, a0:a1], in0=bank[:, a0:a1],
                                                  scalar=cq[:, t, bass.ds(at(hh, 4, r), 1)], in1=bias[:, hh % 2, a0:a1],
                                                  op0=ALU.add, op1=ALU.add)
                fenced(ins, s_scr, at(hh + 1, 4, r))
                ve.tensor_reduce(rmax[:, 0:1], probs[:, 0:P], AX_X, ALU.max)
                link(ve.tensor_reduce(rmax[:, 1:2], probs[:, P:3 * P], AX_X, ALU.max))
                fenced(ve.tensor_scalar(nmax, rmax, -1.0, None, ALU.mult), s_mx, at(hh + 1, 4, r))

            def head_probs(hh, r=0):
                ve.wait_ge(s_exp, at(hh + 1, 4, r))
                link(ve.reciprocal(rinv, rsum))
                ve.tensor_scalar(probs[:, 0:P], probs[:, 0:P], rinv[:, 0:1], None, ALU.mult)
                fenced(ve.tensor_scalar(probs[:, P:3 * P], probs[:, P:3 * P], rinv[:, 1:2], None, ALU.mult),
                       s_pr, at(hh + 1, 4, r))

            def head_low(hh, bank, r=0):
                ve.wait_ge(s_atthi, at(hh + 1, 4, r))
                y = bass.ds(at(hh, 4, r), 1)
                fenced(ve.tensor_tensor(Y[:, y, TOK:].rearrange("p a t -> p (a t)"), bank[:, 0:TOK],
                                        Y[:, y, 0:TOK].rearrange("p a t -> p (a t)").bitcast(F32), ALU.subtract),
                       s_attlo, at(hh + 1, 4, r))

            def heads_of_group(first, r=0):
                c, hh = N_MIX1 + 12 * first, 4 * first
                for k in range(12):
                    if first == 0 and k == 0:
                        turned_low(2, 2)
                        turned_low(2, 3)
                        mean_square(2)
                        spread_rstd(2)
                    if first and k in (1, 3, 5):
                        head_low(hh - 3 + k // 2, psA[:, 3, :], r)
                    if first and k in (1, 3):
                        head_logits(hh - 2 + k // 2, psA[:, 2, :], r)
                        head_probs(hh - 2 + k // 2, r)
                    if k == 11:
                        head_low(hh, psA[:, 3, :], r)
                    if k in (9, 11):
                        head_logits(hh + (k - 9) // 2, psA[:, 2, :], r)
                        head_probs(hh + (k - 9) // 2, r)
                    low(c + k + LEAD, r)
                    if first == 0 and k == 1:
                        take_rstd(2)
                        link(ve.tensor_scalar(q_rstdT, rstdT[:, :], float(P) ** -0.5, None, ALU.mult))
                    if first == 0 and k == 2:
                        ve.wait_ge(s_ft, 1)
                        for t in range(2):
                            link(ve.scalar_tensor_tensor(out=fl[:, t, :], in0=psA[:, 2, 16 * t:16 * t + 16],
                                                         scalar=rstd[:, t:t + 1], in1=bf, op0=ALU.mult, op1=ALU.add))
                        fenced(ve.scalar_tensor_tensor(out=fe, in0=fl, scalar=-1.0, in1=fl, op0=ALU.mult, op1=ALU.min),
                               s_fl, 1)
                    if first == 0 and k == 3:
                        ve.wait_ge(s_fe, 1)
                        fenced(ve.scalar_tensor_tensor(out=lf, in0=fl, scalar=0.0, in1=fe, op0=ALU.min, op1=ALU.subtract),
                               s_lf, 1)
                    if first == 0 and k == 4:
                        ve.wait_ge(s_c, 1)
                        link(ve.tensor_copy(cq, psA[:, 2, 0:32].rearrange("p (t h) -> p t h", t=2)))
                        fenced(ve.tensor_scalar(cneg, psA[0:HEADS, 3, 0:TOK], -1.0, None, ALU.mult), s_cq, 1)
                    if k in (5, 7, 9, 11):
                        take_qk((k - 5) // 2, first, r)

            heads_of_group(0)
            with ve.Fori(0, 3) as r:
                before = chain["n"]
                chain.update(r=r, step=HEAD_LINKS)
                heads_of_group(1, r)
                assert chain["n"] == before + HEAD_LINKS, chain["n"] - before
                chain.update(n=before + HEAD_LINKS * 3, r=0, step=0)
            for k in range(16):
                if k == 1:
                    head_low(13, psT[:, 1, :])
                if k in (3, 5):
                    head_low(13 + k // 2, psT[:, 3, :])
                if k in (1, 3):
                    head_logits(14 + k // 2, psT[:, 2, :])
                    head_probs(14 + k // 2)
                if k in (8, 9, 13):
                    turned_low(3, {8: 0, 9: 1, 13: 2}[k])
                low(N_OUT1 + k + LEAD)
                if k in (6, 7, 11, 15):
                    c = {6: 0, 7: 1, 11: 2, 15: 3}[k]
                    add_to_x(A_OUT1 + c, c, N_OUT1 + k)
            ffn(1)

            times_gain(2)
            for t in range(2):
                if t == 0:
                    ve.wait_ge(s_tile0, 1)
                else:
                    ve.wait_ge(s_used, N_END)
                xc = x[:, t, D - 512:D]
                fenced(ve.tensor_tensor(xc, xc, psA[:, 2 + t, :], ALU.add), s_xlast, t + 1)
                link(ve.tensor_tensor(last_g[:, t, :], xc, final_g[:, D - 512:D], ALU.mult))
            mean_square(4)
            ve.wait_ge(s_sd, 5)
            refined_rsqrt(rstd, ms, sd, rr, nt, last=s_final)
            for n in range(4):
                xc = x[:, 0, 512 * n:512 * n + 512]
                ve.tensor_scalar(xc, last_g[:, 0, :] if n == 3 else xc, rstd[:, 0:1], None, ALU.mult)\
                    .then_inc(s_fin0, 1)

        @block.tensor
        def _(pe):
            def turned_half(c, k, slot, acts, r=0):
                s = c % RING
                hi = wh[:, s, :].rearrange("p (k n) -> p k n", k=8)
                lo = wl[:, s, :].rearrange("p (k n) -> p k n", k=8)
                pe.wait_ge(s_low, at(c + 1, 12, r))
                for m in range(2):
                    bank = psT[:, 2 * slot + m, :]
                    for kk in range(8):
                        K = 8 * k + kk
                        pe.matmul(bank, hi[:, kk, P * m:P * m + P], acts[:, K, :], start=(K == 0), stop=False,
                                  skip_group_check=True)
                        ins = pe.matmul(bank[:, TOK:], lo[:, kk, P * m:P * m + P], acts[:, K, 0:TOK], start=False,
                                        stop=(K == KC - 1), skip_group_check=True)
                ins.then_inc(s_used, 1)

            def straight_quad(c, slot, acts, k0, first, last, r=0, tile0=None):
                s = c % RING
                hi = wh[:, s, :].rearrange("p (k n) -> p k n", k=4)
                lo = wl[:, s, :].rearrange("p (k n) -> p k n", k=4)
                pe.wait_ge(s_low, at(c + 1, 12, r))
                for t in range(2):
                    bank = psA[:, 2 * slot + t, :]
                    for kk in range(4):
                        ah = acts[:, k0 + kk, P * t:P * t + P]
                        al = acts[:, k0 + kk, TOK + P * t:TOK + P * t + P]
                        pe.matmul(bank, ah, hi[:, kk, :], start=(first and kk == 0), stop=False)
                        pe.matmul(bank, ah, lo[:, kk, :], start=False, stop=False)
                        ins = pe.matmul(bank, al, hi[:, kk, :], start=False, stop=(last and kk == 3))
                    if t == 0 and tile0 is not None:
                        ins.then_inc(tile0, 1)
                ins.then_inc(s_used, 1)

            def transpose_x(s, n):
                if n < 2:
                    if s:
                        pe.wait_ge(s_added, Q_READY[s])
                        if s == 3:
                            pe.wait_ge(s_attlo, HEADS)
                else:
                    pe.wait_ge(s_turned, 4 * s + n - 1)
                if s:
                    pe.wait_ge(s_xadd, X_READY[s] + n + 1)
                else:
                    pe.wait_ge(s_x[n], 16)
                for kk in range(4):
                    for t in range(2):
                        ins = pe.transpose(turned_bank(s, n, kk)[:, P * t:P * t + P],
                                           x[:, t, 512 * n + P * kk:512 * n + P * kk + P], ident[:, :])
                ins.then_inc(s_turn, 1)

            def spread(s):
                pe.wait_ge(s_diag, s + 1)
                bank = psA[:, 3, :] if s else psT[:, 1, :]
                for t in range(2):
                    ins = pe.matmul(bank[:, P * t:P * t + P], ones[:, :], diag[:, t, :], start=(t == 0), stop=True,
                                    skip_group_check=True)
                ins.then_inc(s_bc, 1)

            pe.wait_ge(s_const, 3)
            transpose_x(0, 0)
            pe.wait_ge(s_gains, 16)
            pe.transpose(psA[:, 2, 0:32], rows[0:32, :], ident[0:32, 0:32]).then_inc(s_vec, 1)
            transpose_x(0, 1)

            for c in range(2):
                for q in range(4):
                    n = N_V0 + 4 * c + q
                    if c == 0:
                        pe.wait_ge(s_turned, q + 1)
                    straight_quad(n, c, H, 4 * q, q == 0, q == 3)
                    if n in (0, 1):
                        transpose_x(0, n + 2)
                    if n == 3:
                        pe.wait_ge(s_rows, 16 * 4)
                        pe.transpose(psT[:, 2, 8 * FT:8 * FT + 88], rows, ident[0:88, 0:88])
                        pe.wait_ge(s_conv, 16 * 4)
                        for l in range(2):
                            for j in range(4):
                                ins = pe.transpose(psT[:, 2 + l, 2 * FT * j:2 * FT * j + 2 * FT], conv_rows[:, l, j, :],
                                                   ident[0:2 * FT, 0:2 * FT])
                            ins.then_inc(s_vec, 1)
                        pe.wait_ge(s_sp, 16)
                        for g in range(AG):
                            ins = pe.transpose(psT[:, 0, P * g:P * g + P], w_sp[:, g, :], ident[:, :])
                        ins.then_inc(s_spT, 1)
                    if n == 4:
                        spread(0)
                    if n == 5:
                        pe.wait_ge(s_WT, 1)
                        pe.matmul(psT[:, 0, :], ones[:, :], WT.rearrange("p g t -> p (g t)"), start=True, stop=True)\
                            .then_inc(s_wsum, 1)
            pe.wait_ge(s_wsr, 1)
            for j in range(4):
                for k in range(2):
                    if j >= 2 and k == 0:
                        pe.wait_ge(s_added, Q_POOL + j - 1)
                    turned_half(N_POOL + 2 * j + k, k, j % 2, H)

            def pool_product(g):
                s = N_WPOOL % RING
                hi = wh[:, s, :].rearrange("p (k n) -> p k n", k=8)
                lo = wl[:, s, :].rearrange("p (k n) -> p k n", k=8)
                if g == 0:
                    pe.wait_ge(s_low, N_WPOOL + 1)
                    pe.wait_ge(s_z, 2)
                if g >= 2:
                    pe.wait_ge(s_added, Q_WPOOL + g - 1)
                pe.wait_ge(s_plo, g + 1)
                for m in range(2):
                    bank = psA[:, 2 * (g % 2) + m, :]
                    for kk in range(2):
                        K = 2 * g + kk
                        pe.matmul(bank, hi[:, K, P * m:P * m + P], Y[:, K, :], start=(kk == 0), stop=False,
                                  skip_group_check=True)
                        ins = pe.matmul(bank[:, TOK:], lo[:, K, P * m:P * m + P], Y[:, K, 0:TOK], start=False,
                                        stop=(kk == 1), skip_group_check=True)
                ins.then_inc(s_wp if g < 3 else s_used, 1)

            for j in range(4):
                for k in range(2):
                    if j == 1:
                        pool_product(2 * k)
                        pool_product(2 * k + 1)
                    if k == 0:
                        pe.wait_ge(s_added, [Q_POOL + 3, Q_POOL + 4, Q_U[0] + 1, Q_U[1] + 1][j])
                    turned_half(N_U[j][k], k, j % 2, H)
                if j == 1:
                    pe.wait_ge(s_zn, 1)
                    pe.wait_ge(s_added, Q_WPOOL + 4)
                    for g in range(AG):
                        for m in range(2):
                            for b in range(2):
                                c0 = TOK * m + P * b
                                ins = pe.matmul(psA[:, g, c0:c0 + P], z[:, b, GD * g + P * m:GD * g + P * m + P],
                                                WT[:, g, :], start=(c0 == 0), stop=True, skip_group_check=True)
                    ins.then_inc(s_gate, 1)
            for n, (c, q) in enumerate(OUT0_ORDER):
                if n in (0, 4):
                    pe.wait_ge(s_ya, 2 + n // 2)
                if c >= 2 and n % 4 == 0:
                    pe.wait_ge(s_xadd, A_OUT0 + c - 1)
                if c == 0:
                    pe.wait_ge(s_yblo if q >= 2 else s_yalo, 2 * (q % 2) + 2)
                straight_quad(N_OUT0 + n, c % 2, Y, 4 * q, n % 4 == 0, n % 4 == 3)
                if n in (4, 8, 12):
                    transpose_x(1, n // 4 - 1)

            def panel(l, g, j, c, r=0):
                q = Q_FFN[l] + 4 * g + j
                if g or j >= 2 or not isinstance(r, int):
                    pe.wait_ge(s_added, at(q - 1, 4, r))
                for k in range(2):
                    turned_half(c + k, k, j % 2, H, r)

            def down(l, g, c, r=0, frm=0, transposes=False):
                if frm:
                    pe.wait_ge(s_actlo, 22 * l + 2 * g + 2)
                else:
                    pe.wait_ge(s_actlo, at(22 * l + 2 * g + 2, 2, r))
                for n in range(4):
                    i = A_FFN[l] + 4 * g + n
                    pe.wait_ge(s_xadd, at(i - 1, 4, r))
                    final = l == 1 and frm and n == 3
                    straight_quad(c + n, n % 2, Y, 4 * frm, True, True, r, tile0=s_tile0 if final else None)
                    if transposes and n >= 1:
                        transpose_x(2, n - 1)

            def ffn(l):
                B, s = N_FFN[l], 1 + 2 * l
                pe.wait_ge(s_turned, 4 * s + 3)
                turned_half(B, 0, 0, H)
                transpose_x(s, 3)
                turned_half(B + 1, 0, 1, H)
                pe.wait_ge(s_turned, 4 * s + 4)
                turned_half(B + 2, 1, 0, H)
                spread(s)
                turned_half(B + 3, 1, 1, H)
                for j in range(2, 4):
                    panel(l, 0, j, B + 2 * j)
                pe.wait_ge(s_rstd, s + 1)
                with pe.Fori(0, NG - 2) as r:
                    panel(l, 1, 0, B + 8, r)
                    panel(l, 1, 1, B + 10, r)
                    down(l, 0, B + 12, r)
                    panel(l, 1, 2, B + 16, r)
                    panel(l, 1, 3, B + 18, r)
                for j in range(4):
                    panel(l, NG - 1, j, B + 116 + 2 * j)
                down(l, NG - 2, B + 124)
                down(l, NG - 1, B + 128, frm=1, transposes=(l == 0))

            ffn(0)

            def scores(hh, bank, group, r=0):
                if isinstance(r, int) and hh == 0:
                    pe.wait_ge(s_cq, 1)
                else:
                    pe.wait_ge(s_scr, at(hh, 4, r))
                pair = (hh // 2) % 2
                pe.wait_ge(s_qk, at(4 * group + 2 * pair + 2, 4, r))
                qT, kT = qk[pair]
                m = hh % 2
                pe.matmul(bank[:, 0:P], qT[:, m, 0:P], kT[:, m, 0:P], start=True, stop=True, skip_group_check=True)
                pe.matmul(bank[:, P:3 * P], qT[:, m, P:TOK], kT[:, m, :], start=False, stop=True,
                          skip_group_check=True).then_inc(s_sc, 1)

            def turn_probs(hh, bank, r=0):
                pe.wait_ge(s_pr, at(hh + 1, 4, r))
                if not (isinstance(r, int) and hh == 0):
                    pe.wait_ge(s_attlo, at(hh, 4, r))
                for b in range(3):
                    ins = pe.transpose(bank[:, P * b:P * b + P], probs[:, P * b:P * b + P], ident[:, :])
                ins.then_inc(s_pt, 1)

            def attend(hh, bank, group, r=0):
                pe.wait_ge(s_ptc, at(hh + 1, 4, r))
                pe.wait_ge(s_vr, at(group + 1, 1, r))
                f = P * (hh % 4)
                pe.matmul(bank[:, 0:TOK], v[:, 0, f:f + P], probsT[:, 0:TOK], start=True, stop=False,
                          skip_group_check=True)
                pe.matmul(bank[:, P:TOK], v[:, 1, f:f + P], probsT[:, TOK:3 * P], start=False, stop=True,
                          skip_group_check=True).then_inc(s_att, 1)

            def forget_sums():
                pe.wait_ge(s_wfs, 2)
                wfh = wf_split[:, 0, :].rearrange("p (k h) -> p k h", k=KC)
                wfl = wf_split[:, 1, :].rearrange("p (k h) -> p k h", k=KC)
                for k in range(KC):
                    pe.matmul(psA[0:HEADS, 2, :], wfh[:, k, :], H[:, k, :], start=(k == 0), stop=False,
                              skip_group_check=True)
                    ins = pe.matmul(psA[0:HEADS, 2, TOK:], wfl[:, k, :], H[:, k, 0:TOK], start=False,
                                    stop=(k == KC - 1), skip_group_check=True)
                ins.then_inc(s_f, 1)

            def turn_forget_sums():
                pe.wait_ge(s_fT, 1)
                for t in range(2):
                    for part in range(2):
                        c0 = TOK * part + P * t
                        ins = pe.matmul(psA[:, 2, HEADS * t:HEADS * t + HEADS], fT[:, c0:c0 + P],
                                        ident[0:HEADS, 0:HEADS], start=(part == 0), stop=(part == 1),
                                        skip_group_check=True)
                ins.then_inc(s_ft, 1)

            def cumulate():
                pe.wait_ge(s_lf, 1)
                pe.wait_ge(s_const, 6)
                c0, c1 = psA[:, 2, 0:HEADS], psA[:, 2, HEADS:2 * HEADS]
                pe.matmul(c0, tri, lf[:, 0, :], start=True, stop=True)
                pe.matmul(c1, ones[:, :], lf[:, 0, :], start=True, stop=False)
                pe.matmul(c1, tri, lf[:, 1, :], start=False, stop=True)
                r0, r1 = psA[0:HEADS, 3, 0:P], psA[0:HEADS, 3, P:TOK]
                pe.matmul(r0, lf[:, 0, :], tri, start=True, stop=True)
                pe.matmul(r1, lf[:, 0, :], ones[:, :], start=True, stop=False)
                pe.matmul(r1, lf[:, 1, :], tri, start=False, stop=True).then_inc(s_c, 1)

            SB, AB = psA[:, 2, :], psA[:, 3, :]

            def heads_of_group(first, r=0):
                c, hh = N_MIX1 + 12 * first, 4 * first
                for k in range(12):
                    if k < 4:
                        if first == 0:
                            pe.wait_ge(s_turned, 8 + k + 1)
                            if k == 0:
                                pe.wait_ge(s_xadd, A_FFN[0] + 4 * NG - 1)
                        elif k == 0:
                            pe.wait_ge(s_vr, at(first, 1, r))
                        straight_quad(c + k, 0, H, 4 * k, k == 0, k == 3, r)
                    else:
                        j = (k - 4) // 2
                        q = Q_MIX1 + 4 * first + j
                        if k % 2 == 0:
                            if first or j >= 2:
                                pe.wait_ge(s_added, at(q - 1, 4, r))
                            else:
                                pe.wait_ge(s_turned, 12)
                        turned_half(c + k, k % 2, j % 2, H, r)
                    if first == 0 and k == 0:
                        transpose_x(2, 3)
                    if first == 0 and k == 1:
                        spread(2)
                        forget_sums()
                    if first == 0 and k == 2:
                        turn_forget_sums()
                    if first == 0 and k == 4:
                        cumulate()
                    if first and k in (0, 2, 4):
                        attend(hh - 3 + k // 2, AB, first - 1, r)
                    if first and k in (0, 2):
                        scores(hh - 2 + k // 2, SB, first - 1, r)
                    if first and k in (1, 3):
                        turn_probs(hh - 2 + k // 2, AB, r)
                    if k == 10:
                        attend(hh, AB, first, r)
                    if k in (8, 10):
                        scores(hh + (k - 8) // 2, SB, first, r)
                    if k in (9, 11):
                        turn_probs(hh + (k - 9) // 2, AB, r)

            heads_of_group(0)
            with pe.Fori(0, 3) as r:
                heads_of_group(1, r)
            for n, (c, q) in enumerate(OUT1_ORDER):
                if n == 0:
                    pe.wait_ge(s_vr, 4)
                if n == 3:
                    pe.wait_ge(s_scr, 14)
                    pe.wait_ge(s_ptc, 14)
                if c >= 2 and q == 0:
                    pe.wait_ge(s_xadd, A_OUT1 + c - 1)
                if c < 2:
                    pe.wait_ge(s_attlo, 4 * q + 4)
                straight_quad(N_OUT1 + n, c % 2, Y, 4 * q, q == 0, q == 3)
                if n == 0:
                    pe.wait_ge(s_qk, 16)
                    attend(13, psT[:, 1, :], 3)
                if n in (0, 2):
                    scores(14 + n // 2, psT[:, 2, :], 3)
                if n in (1, 3):
                    turn_probs(14 + n // 2, psT[:, 3, :])
                if n in (2, 4):
                    attend(13 + n // 2, psT[:, 3, :], 3)
                if n in (7, 8, 12):
                    transpose_x(3, {7: 0, 8: 1, 12: 2}[n])
            ffn(1)


NAMES = ["x", "norm_mix_g", "norm_ffn_g", "final_norm_g", "w_in_even", "ln_v_g", "ln_v_b", "w_spatial", "b_spatial",
         "w_pool", "pool_scale", "w_out_even", "w_in_odd", "b_forget", "w_out_odd", "w_up", "conv_w", "conv_b", "w_down"]


def kernel(**inputs):
    import numpy as np
    import concourse.bacc as bacc
    from concourse.bass_utils import run_bass_kernel_spmd

    nc = bacc.Bacc("TRN2", target_bir_lowering=False, num_devices=1)
    arrays, args = {}, []
    for name in NAMES:
        a = np.ascontiguousarray(inputs[name])
        arrays[f"in_{name}"] = a
        args.append(nc.dram_tensor(f"in_{name}", a.shape, mybir.dt.from_np(a.dtype), kind="ExternalInput").ap())
    result = nc.dram_tensor("result", arrays["in_x"].shape, F32, kind="ExternalOutput").ap()
    c_dram = nc.dram_tensor("c_rows", (arrays["in_b_forget"].shape[1], arrays["in_x"].shape[1]), F32,
                            kind="Internal").ap()
    build(nc, *args, result, c_dram)
    r = run_bass_kernel_spmd(nc, [arrays], core_ids=[0])
    return r.results[0]["result"]
```
